# Optimizing a Trainium2 kernel written in Bass

```python
import jax, jax.numpy as jnp
from jax import lax
import numpy as np

D_MODEL = 2048
BATCH = 1
SEQ = 256
DEPTH = 2

EXPAND = 2
D_INNER = EXPAND * D_MODEL
PLE_DIM = 256
N_MIXERS = 2
POOL_WINDOWS = (2, 4, 8, 16)
N_POOL_GROUPS = len(POOL_WINDOWS)
POOL_GROUP_DIM = D_INNER // N_POOL_GROUPS
LRU_HEADS = 16
LRU_BLOCK = D_INNER // LRU_HEADS
CONV_WIDTH = 4
LRU_C = 8.0
RMS_EPS = 1e-6
N_POOL_LAYERS = (DEPTH + 1) // 2
N_LRU_LAYERS = DEPTH // 2


def rmsnorm(x, g):
    xf = x.astype(jnp.float32)
    var = jnp.mean(xf * xf, axis=-1, keepdims=True)
    return (xf * lax.rsqrt(var + RMS_EPS) * g.astype(jnp.float32)).astype(x.dtype)

def pool_mixer(u, w_grp, b, scale):
    B, S, E = u.shape
    maxw = POOL_WINDOWS[-1]
    uf = u.astype(jnp.float32)
    cs = jnp.cumsum(uf, axis=1)
    csp = jnp.pad(cs, ((0, 0), (maxw, 0), (0, 0)))
    pos = jnp.arange(1, S + 1, dtype=jnp.int32)
    diffs = []
    for g, w in enumerate(POOL_WINDOWS):
        c0, c1 = g * POOL_GROUP_DIM, (g + 1) * POOL_GROUP_DIM
        win_sum = csp[:, maxw:, c0:c1] - csp[:, maxw - w:maxw - w + S, c0:c1]
        count = jnp.minimum(pos, w).astype(jnp.float32)[None, :, None]
        diffs.append(win_sum / count - uf[..., c0:c1])
    d = jnp.stack(diffs, axis=2).astype(u.dtype)
    y = jnp.einsum('bsgc,gcd->bsgd', d, w_grp).reshape(B, S, E) + b
    return y * scale

def causal_depthwise_conv(x, w, b):
    S = x.shape[1]
    xp = jnp.pad(x, ((0, 0), (CONV_WIDTH - 1, 0), (0, 0)))
    y = b
    for k in range(CONV_WIDTH):
        y = y + xp[:, k:k + S] * w[k]
    return y

def rglru(x, wa, ba, wx, bx, lam):
    B, S, E = x.shape
    xb = x.reshape(B, S, LRU_HEADS, LRU_BLOCK)
    r = jax.nn.sigmoid((jnp.einsum('bshi,hij->bshj', xb, wa).reshape(B, S, E) + ba).astype(jnp.float32))
    ig = jax.nn.sigmoid((jnp.einsum('bshi,hij->bshj', xb, wx).reshape(B, S, E) + bx).astype(jnp.float32))
    log_a = -LRU_C * r * jax.nn.softplus(-lam.astype(jnp.float32))
    a = jnp.exp(log_a)
    mult = jnp.sqrt(jnp.maximum(-jnp.expm1(2.0 * log_a), 0.0))
    bterm = mult * ig * x.astype(jnp.float32)

    def combine(left, right):
        a1, b1 = left
        a2, b2 = right
        return a1 * a2, a2 * b1 + b2

    _, h = lax.associative_scan(combine, (a, bterm), axis=1)
    return h.astype(x.dtype)

def first_inputs(seed: int = 0) -> dict:
    key = jax.random.key(seed)
    ks = jax.random.split(key, 24)
    f32 = jnp.float32

    def nrm(k, shape, fan_in):
        return jax.random.normal(k, shape, f32) * (fan_in ** -0.5)

    def gain(k, shape):
        return 1.0 + 0.05 * jax.random.normal(k, shape, f32)

    def bias(k, shape):
        return 0.01 * jax.random.normal(k, shape, f32)

    a0 = jax.random.uniform(ks[15], (N_LRU_LAYERS, D_INNER), f32, 0.9, 0.999)
    lru_L = jnp.log(a0) - jnp.log1p(-a0)
    return {
        "x": jax.random.normal(ks[0], (BATCH, SEQ, D_MODEL), f32),
        "p": jax.random.normal(ks[1], (DEPTH, BATCH, SEQ, PLE_DIM), f32),
        "w_in": nrm(ks[2], (DEPTH, D_MODEL, 2 * D_INNER), D_MODEL),
        "w_out": nrm(ks[3], (DEPTH, D_INNER, D_MODEL), D_INNER),
        "g_pre": gain(ks[4], (DEPTH, D_MODEL)),
        "g_post": gain(ks[5], (DEPTH, D_MODEL)),
        "pool_w": nrm(ks[6], (N_POOL_LAYERS, N_POOL_GROUPS, POOL_GROUP_DIM, POOL_GROUP_DIM), POOL_GROUP_DIM),
        "pool_b": bias(ks[7], (N_POOL_LAYERS, D_INNER)),
        "pool_scale": gain(ks[8], (N_POOL_LAYERS, D_INNER)),
        "conv_w": nrm(ks[9], (N_LRU_LAYERS, CONV_WIDTH, D_INNER), CONV_WIDTH),
        "conv_b": bias(ks[10], (N_LRU_LAYERS, D_INNER)),
        "lru_wa": nrm(ks[11], (N_LRU_LAYERS, LRU_HEADS, LRU_BLOCK, LRU_BLOCK), LRU_BLOCK),
        "lru_ba": bias(ks[12], (N_LRU_LAYERS, D_INNER)),
        "lru_wx": nrm(ks[13], (N_LRU_LAYERS, LRU_HEADS, LRU_BLOCK, LRU_BLOCK), LRU_BLOCK),
        "lru_bx": bias(ks[14], (N_LRU_LAYERS, D_INNER)),
        "lru_L": lru_L,
        "w_ple": nrm(ks[16], (DEPTH, PLE_DIM, D_MODEL), PLE_DIM),
        "w_ple_gate": nrm(ks[17], (DEPTH, D_MODEL, D_MODEL), D_MODEL),
        "g_ple_in": gain(ks[18], (DEPTH, D_MODEL)),
        "g_ple_out": gain(ks[19], (DEPTH, D_MODEL)),
    }

def first_block(x, p, w_in, w_out, g_pre, g_post, pool_w, pool_b, pool_scale,
              conv_w, conv_b, lru_wa, lru_ba, lru_wx, lru_bx, lru_L,
              w_ple, w_ple_gate, g_ple_in, g_ple_out):
    for i in range(DEPTH):
        h = rmsnorm(x, g_pre[i])
        uz = jnp.einsum('bsd,de->bse', h, w_in[i])
        u, z = uz[..., :D_INNER], uz[..., D_INNER:]
        j = i // N_MIXERS
        if i % N_MIXERS == 0:
            y = pool_mixer(u, pool_w[j], pool_b[j], pool_scale[j])
        else:
            uc = causal_depthwise_conv(u, conv_w[j], conv_b[j])
            y = rglru(uc, lru_wa[j], lru_ba[j], lru_wx[j], lru_bx[j], lru_L[j])
        y = y * jax.nn.silu(z)
        o = jnp.einsum('bse,ed->bsd', y, w_out[i])
        x = x + rmsnorm(o, g_post[i])
        gate = jax.nn.sigmoid(jnp.einsum('bsd,de->bse', rmsnorm(x, g_ple_in[i]), w_ple_gate[i]))
        e = jnp.einsum('bsk,kd->bsd', p[i], w_ple[i])
        x = x + rmsnorm(e * gate, g_ple_out[i])
    return x


MLA_HEADS = 8
MLA_NOPE = 128
MLA_ROPE = 64
MLA_QK = MLA_NOPE + MLA_ROPE
MLA_V = 128
MLA_Q_RANK = 512
MLA_KV_RANK = 512
MLA_WIDTH = MLA_HEADS * MLA_V
ROPE_THETA = 10000.0
Q_BLOCK = 128
SGU_GROUPS = 8
SGU_CHUNK = 128
SGU_WIDTH = 1024
SGU_GROUP_DIM = SGU_WIDTH // SGU_GROUPS
GLA_HEADS = 4
GLA_DK = 128
GLA_DV = 256
GLA_GATE_RANK = 16
GLA_TAU = 16.0
GLA_CHUNK = 128
GLA_WIDTH = GLA_HEADS * GLA_DV
N_BRANCH = 3
BRANCH_WIDTH = 1024
EPS = 1e-6

IN_SIZES = (MLA_Q_RANK, MLA_KV_RANK, MLA_ROPE, MLA_WIDTH,
            SGU_WIDTH, SGU_WIDTH, SGU_WIDTH,
            GLA_HEADS * GLA_DK, GLA_HEADS * GLA_DK, GLA_WIDTH, GLA_GATE_RANK, GLA_WIDTH,
            N_BRANCH * D_MODEL)
IN_COLS = sum(IN_SIZES)
IN_SPLITS = tuple(int(c) for c in np.cumsum(IN_SIZES)[:-1])


def rms_norm(x, g):
    xf = x.astype(jnp.float32)
    y = xf * lax.rsqrt(jnp.mean(xf * xf, axis=-1, keepdims=True) + EPS)
    return (y * g.astype(jnp.float32)).astype(x.dtype)

def rope_tables(positions, dtype):
    inv_freq = 1.0 / (ROPE_THETA ** (jnp.arange(0, MLA_ROPE, 2, dtype=jnp.float32) / MLA_ROPE))
    ang = positions.astype(jnp.float32)[..., None] * inv_freq
    return jnp.cos(ang).astype(dtype)[:, :, None, :], jnp.sin(ang).astype(dtype)[:, :, None, :]

def apply_rope(x, cos, sin):
    half = x.shape[-1] // 2
    x1, x2 = x[..., :half], x[..., half:]
    return jnp.concatenate([x1 * cos - x2 * sin, x2 * cos + x1 * sin], axis=-1)

def causal_block_attention(q, k, v):
    S = q.shape[1]
    scale = MLA_QK ** -0.5
    neg = jnp.finfo(jnp.float32).min
    outs = []
    for i in range(S // Q_BLOCK):
        q0, q1 = i * Q_BLOCK, (i + 1) * Q_BLOCK
        qb, kb, vb = q[:, q0:q1], k[:, :q1], v[:, :q1]
        s = jnp.einsum('bqhd,bkhd->bhqk', qb, kb).astype(jnp.float32) * scale
        mask = (q0 + jnp.arange(Q_BLOCK))[:, None] >= jnp.arange(q1)[None, :]
        p = jax.nn.softmax(jnp.where(mask, s, neg), axis=-1).astype(v.dtype)
        outs.append(jnp.einsum('bhqk,bkhd->bqhd', p, vb))
    return jnp.concatenate(outs, axis=1)

def mla_branch(c_q, c_kv, k_rope, cq_g, ckv_g, w_uq, w_ukv, q_g, k_g, cos, sin):
    B, S, _ = c_q.shape
    q = (rms_norm(c_q, cq_g) @ w_uq).reshape(B, S, MLA_HEADS, MLA_QK)
    kv = (rms_norm(c_kv, ckv_g) @ w_ukv).reshape(B, S, MLA_HEADS, MLA_NOPE + MLA_V)
    k_nope, v = kv[..., :MLA_NOPE], kv[..., MLA_NOPE:]
    k = jnp.concatenate([k_nope, jnp.broadcast_to(k_rope[:, :, None, :], (B, S, MLA_HEADS, MLA_ROPE))], axis=-1)
    q = rms_norm(q, q_g)
    k = rms_norm(k, k_g)
    q = jnp.concatenate([q[..., :MLA_NOPE], apply_rope(q[..., MLA_NOPE:], cos, sin)], axis=-1)
    k = jnp.concatenate([k[..., :MLA_NOPE], apply_rope(k[..., MLA_NOPE:], cos, sin)], axis=-1)
    o = causal_block_attention(q, k, v)
    return o.reshape(B, S, MLA_WIDTH)

def sgu_branch(u, v, v_g, w_s, b_s):
    B, S, _ = u.shape
    nc = S // SGU_CHUNK
    v = rms_norm(v, v_g).reshape(B, nc, SGU_CHUNK, SGU_GROUPS, SGU_GROUP_DIM)
    mix = jnp.einsum('gts,bcsgd->bctgd', jnp.tril(w_s), v) + b_s.T[:, :, None]
    return u * mix.reshape(B, S, SGU_WIDTH)

def gla_branch(q, k, v, a_r, w_a2, b_a, o_g):
    B, S, _ = q.shape
    nc = S // GLA_CHUNK
    L = GLA_CHUNK
    log_a = jax.nn.log_sigmoid((a_r @ w_a2 + b_a).astype(jnp.float32)) / GLA_TAU

    def chunks(t, d):
        return t.reshape(B, nc, L, GLA_HEADS, d).transpose(1, 0, 3, 2, 4)

    qc = chunks(q.astype(jnp.float32) * GLA_DK ** -0.5, GLA_DK)
    kc = chunks(k.astype(jnp.float32), GLA_DK)
    vc = chunks(v.astype(jnp.float32), GLA_DV)
    bc = jnp.cumsum(chunks(log_a, GLA_DK), axis=3)
    mask = jnp.tril(jnp.ones((L, L), dtype=bool))[:, :, None]

    def step(state, inp):
        q_, k_, v_, b_ = inp
        o_inter = jnp.einsum('bhtk,bhkv->bhtv', q_ * jnp.exp(b_), state)
        diff = b_[:, :, :, None, :] - b_[:, :, None, :, :]
        decay = jnp.where(mask, jnp.exp(jnp.where(mask, diff, 0.0)), 0.0)
        attn = jnp.einsum('bhtk,bhtsk,bhsk->bhts', q_, decay, k_)
        o = o_inter + jnp.einsum('bhts,bhsv->bhtv', attn, v_)
        b_last = b_[:, :, -1:, :]
        new_state = jnp.exp(b_last[:, :, 0, :])[..., None] * state + \
            jnp.einsum('bhsk,bhsv->bhkv', k_ * jnp.exp(b_last - b_), v_)
        return new_state, o

    state0 = jnp.zeros((B, GLA_HEADS, GLA_DK, GLA_DV), jnp.float32)
    _, o = lax.scan(step, state0, (qc, kc, vc, bc))
    o = o.transpose(1, 0, 3, 2, 4).reshape(B, S, GLA_HEADS, GLA_DV)
    o = rms_norm(o, o_g).astype(v.dtype)
    return o.reshape(B, S, GLA_WIDTH)

def hybrid_layer(x, cos, sin, norm_g, w_in, cq_g, ckv_g, w_uq, w_ukv, q_g, k_g,
                 v_g, w_s, b_s, w_a2, b_a, o_g, w_branch, w_out):
    B, S, D = x.shape
    h = rms_norm(x, norm_g)
    proj = h @ w_in
    (c_q, c_kv, k_rope, z_a, u_b, v_b, z_b, q_c, k_c, v_c, a_r, z_c, gate_logits) = \
        jnp.split(proj, IN_SPLITS, axis=-1)
    y_a = mla_branch(c_q, c_kv, k_rope, cq_g, ckv_g, w_uq, w_ukv, q_g, k_g, cos, sin) * jax.nn.silu(z_a)
    y_b = sgu_branch(jax.nn.gelu(u_b), jax.nn.gelu(v_b), v_g, w_s, b_s) * jax.nn.silu(z_b)
    y_c = gla_branch(q_c, k_c, v_c, a_r, w_a2, b_a, o_g) * jax.nn.silu(z_c)
    g = jax.nn.sigmoid(gate_logits.astype(jnp.float32)).astype(x.dtype).reshape(B, S, N_BRANCH, D)
    merged = (g[:, :, 0] * (y_a @ w_branch[0])
              + g[:, :, 1] * (y_b @ w_branch[1])
              + g[:, :, 2] * (y_c @ w_branch[2]))
    return x + merged @ w_out

def second_inputs(seed: int = 0) -> dict:
    key = jax.random.key(seed)
    ks = jax.random.split(key, 20)
    f32 = jnp.float32

    def nrm(k, shape, fan_in, mult=1.0):
        return jax.random.normal(k, shape, f32) * (fan_in ** -0.5) * mult

    def gain(k, shape):
        return 1.0 + 0.02 * jax.random.normal(k, shape, f32)

    x = jax.random.normal(ks[0], (BATCH, SEQ, D_MODEL), f32)
    offset = jax.random.randint(ks[1], (BATCH, 1), 0, SEQ, dtype=jnp.int32)
    positions = (offset + jnp.arange(SEQ, dtype=jnp.int32)[None, :]).astype(jnp.int32)
    return {
        "x": x,
        "positions": positions,
        "norm_g": gain(ks[2], (DEPTH, D_MODEL)),
        "w_in": nrm(ks[3], (DEPTH, D_MODEL, IN_COLS), D_MODEL),
        "mla_cq_norm": gain(ks[4], (DEPTH, MLA_Q_RANK)),
        "mla_ckv_norm": gain(ks[5], (DEPTH, MLA_KV_RANK)),
        "mla_w_uq": nrm(ks[6], (DEPTH, MLA_Q_RANK, MLA_HEADS * MLA_QK), MLA_Q_RANK),
        "mla_w_ukv": nrm(ks[7], (DEPTH, MLA_KV_RANK, MLA_HEADS * (MLA_NOPE + MLA_V)), MLA_KV_RANK),
        "mla_q_norm": gain(ks[8], (DEPTH, MLA_QK)),
        "mla_k_norm": gain(ks[9], (DEPTH, MLA_QK)),
        "sgu_v_norm": gain(ks[10], (DEPTH, SGU_WIDTH)),
        "sgu_w_s": nrm(ks[11], (DEPTH, SGU_GROUPS, SGU_CHUNK, SGU_CHUNK), SGU_CHUNK),
        "sgu_b_s": 1.0 + 0.02 * jax.random.normal(ks[12], (DEPTH, SGU_GROUPS, SGU_CHUNK), f32),
        "gla_w_a2": nrm(ks[13], (DEPTH, GLA_GATE_RANK, GLA_HEADS * GLA_DK), GLA_GATE_RANK),
        "gla_b_a": 0.1 * jax.random.normal(ks[14], (DEPTH, GLA_HEADS * GLA_DK), f32),
        "gla_o_norm": gain(ks[15], (DEPTH, GLA_DV)),
        "w_branch": nrm(ks[16], (DEPTH, N_BRANCH, BRANCH_WIDTH, D_MODEL), BRANCH_WIDTH),
        "w_out": nrm(ks[17], (DEPTH, D_MODEL, D_MODEL), D_MODEL, 0.5),
    }

def second_block(x, positions, norm_g, w_in, mla_cq_norm, mla_ckv_norm, mla_w_uq, mla_w_ukv,
              mla_q_norm, mla_k_norm, sgu_v_norm, sgu_w_s, sgu_b_s, gla_w_a2, gla_b_a,
              gla_o_norm, w_branch, w_out):
    cos, sin = rope_tables(positions, x.dtype)
    for l in range(DEPTH):
        x = hybrid_layer(x, cos, sin, norm_g[l], w_in[l], mla_cq_norm[l], mla_ckv_norm[l],
                         mla_w_uq[l], mla_w_ukv[l], mla_q_norm[l], mla_k_norm[l],
                         sgu_v_norm[l], sgu_w_s[l], sgu_b_s[l], gla_w_a2[l], gla_b_a[l],
                         gla_o_norm[l], w_branch[l], w_out[l])
    return x


def setup_inputs(seed=0):
    out = dict(first_inputs(seed))
    for name, value in second_inputs(seed + 1).items():
        if name != "x":
            out[name + "_2"] = value
    return out


def reference(
    x, p, w_in, w_out, g_pre, g_post, pool_w, pool_b, pool_scale, conv_w, conv_b, lru_wa,
    lru_ba, lru_wx, lru_bx, lru_L, w_ple, w_ple_gate, g_ple_in, g_ple_out, positions_2,
    norm_g_2, w_in_2, mla_cq_norm_2, mla_ckv_norm_2, mla_w_uq_2, mla_w_ukv_2, mla_q_norm_2,
    mla_k_norm_2, sgu_v_norm_2, sgu_w_s_2, sgu_b_s_2, gla_w_a2_2, gla_b_a_2, gla_o_norm_2,
    w_branch_2, w_out_2,
):
    x = first_block(
        x, p, w_in, w_out, g_pre, g_post, pool_w, pool_b, pool_scale, conv_w, conv_b, lru_wa,
        lru_ba, lru_wx, lru_bx, lru_L, w_ple, w_ple_gate, g_ple_in, g_ple_out,
    )
    return second_block(
        x, positions_2, norm_g_2, w_in_2, mla_cq_norm_2, mla_ckv_norm_2, mla_w_uq_2,
        mla_w_ukv_2, mla_q_norm_2, mla_k_norm_2, sgu_v_norm_2, sgu_w_s_2, sgu_b_s_2, gla_w_a2_2,
        gla_b_a_2, gla_o_norm_2, w_branch_2, w_out_2,
    )


_drawn_inputs = setup_inputs


def setup_inputs(seed=0):
    import zlib

    import numpy as np

    out = dict(_drawn_inputs(seed))
    spreads = {}
    factors = {'conv_b': 3.203,
     'lru_ba': 8.0,
     'lru_bx': 8.0,
     'g_ple_in': 3.72,
     'norm_g_2': 8.0,
     'mla_cq_norm_2': 8.0,
     'mla_ckv_norm_2': 8.0,
     'mla_w_uq_2': 3.654,
     'mla_q_norm_2': 8.0,
     'mla_k_norm_2': 8.0,
     'sgu_v_norm_2': 8.0,
     'sgu_b_s_2': 8.0,
     'gla_w_a2_2': 5.455,
     'gla_b_a_2': 8.0,
     'gla_o_norm_2': 8.0}
    for name, (base, spread) in spreads.items():
        noise = np.random.default_rng([zlib.crc32(name.encode()), seed]).standard_normal(out[name].shape)
        drawn = base * np.exp(spread * noise) if base else spread * noise
        out[name] = __import__('jax').numpy.asarray(drawn.astype(out[name].dtype))
    for name, factor in factors.items():
        out[name] = (out[name] * factor).astype(out[name].dtype)
    return out
```

```python
from contextlib import ExitStack, contextmanager

import numpy as np

import concourse.bass as bass
from concourse import mybir

P = 128
T = 256
D = 2048
DI = 4096
ND = D // P
NI = DI // P
PLE = 256
NP_ = PLE // P
UNIT_TILES = 8
UNIT = UNIT_TILES * P
SLOTS = 4
LOOKAHEAD = SLOTS - 1
BANKS = 4
EPS = 1e-6
POOL_WINDOWS = (2, 4, 8, 16)
PAD = 16
TAPS = 4
HEADS = 16
A_HEADS, NOPE, ROPE, RANK = 8, 128, 64, 512
QK = NOPE + ROPE
G_HEADS, G_DK, G_TAU, LEVELS = 4, 128, 16.0, 8
S_GROUPS = 8
NEG = -1.0e30
GELU_A, GELU_C = 0.7978845608028654, 0.044715
TWO_PI = (6.28125, 0.0019353071693331003, 1.0253131677018246e-11)
LRU_C = 8.0

F32 = mybir.dt.float32
F32R = mybir.dt.float32r
ALU = mybir.AluOpType
ACT = mybir.ActivationFunctionType


class Product:

    def __init__(self, depth, operand):
        self.depth, self.operand = depth, operand


class Stage:

    def __init__(self, name, products, turns):
        self.name, self.products, self.turns = name, products, turns
        tile = 0
        for p in products:
            p.first_tile = tile
            tile += p.depth
            p.last_unit = (tile - 1) // UNIT_TILES
        assert tile % UNIT_TILES == 0
        self.units = tile // UNIT_TILES
        self.width = len(products)


class Chain:

    def __init__(self, sem):
        self.sem, self.base, self.step, self.turn, self.per = sem, 0, 0, 0, 0

    def link(self, eng, ins):
        ins.then_inc(self.sem, 1)
        self.step += 1
        eng.wait_ge(self.sem, self.base + self.turn * self.per + self.step)

    @contextmanager
    def loop(self, turn, count, per):
        self.base += self.step
        self.step, self.turn, self.per = 0, turn, per
        yield
        assert self.step == per, (self.step, per)
        self.base += count * per
        self.step, self.turn, self.per = 0, 0, 0


def wait(eng, sem, value):
    if not isinstance(value, int) or value > 0:
        eng.wait_ge(sem, value)


CHANNELS = (
    [(f"g_pre{l}", ND) for l in range(2)] + [(f"g_post{l}", ND) for l in range(2)]
    + [(f"g_ple_in{l}", ND) for l in range(2)] + [(f"g_ple_out{l}", ND) for l in range(2)]
    + [("pool_b", NI), ("pool_scale", NI)] + [(f"conv_w{k}", NI) for k in range(TAPS)]
    + [("conv_b", NI), ("lru_ba", NI), ("lru_bx", NI), ("lru_L", NI)]
    + [(f"{k}{l}", n) for l in range(2) for k, n in (
        ("norm_g", ND), ("cq_g", 4), ("ckv_g", 4), ("v_g", 8), ("o_g", 2), ("b_a", 4),
        ("gq_nope", 1), ("gk_nope", 1), ("gq_r1", 1), ("gq_r2", 1), ("gk_r1", 1), ("gk_r2", 1))]
)
COLUMN, _at = {}, 0
for _name, _n in CHANNELS:
    COLUMN[_name] = _at
    _at += _n
N_CHANNELS = _at
TABLES = [("ident", P), ("masks", LEVELS * P), ("tri", P), ("neg", P), ("sel", 4), ("rep1", P),
          ("rep2", P), ("rope_rows", P), ("inv_freq", 1)]
TABLE, _at = {}, 0
for _name, _n in TABLES:
    TABLE[_name] = slice(_at, _at + _n)
    _at += _n
N_TABLES = _at


def build(nc, weights, x_in, p_in, channels, inv_counts, tables, positions, w_a2, w_s, b_s, x_scratch,
          out):
    with ExitStack() as ctx:
        def sb(name, shape, dt=F32, into=ctx):
            return into.enter_context(nc.sbuf_tensor(name, shape, dt))

        def sem(name):
            return ctx.enter_context(nc.semaphore(name))

        raw = sb("raw", [P, SLOTS, UNIT])
        w_hi = sb("w_hi", [P, SLOTS, UNIT], F32R)
        w_lo = sb("w_lo", [P, SLOTS, UNIT], F32R)
        xs = sb("xs", [P, ND, 2 * T], F32R)
        small = sb("small", [P, 2, T])
        val = sb("val", [P, 4, T])
        act = sb("act", [P, 4, T])
        acc = sb("acc", [P, T])
        sq = sb("sq", [P, T])
        rstd_x = sb("rstd_x", [P, T])
        rstd_r = sb("rstd_r", [P, T])
        rms = sb("rms", [P, T])
        mean_d = sb("mean_d", [P, P])
        power = sb("power", [P, 4])
        ones_col, eps_col = power[:, 2:3], power[:, 3:4]
        chan = sb("chan", [P, N_CHANNELS])
        with ExitStack() as temps:
            taps_in = sb("taps_in", [P, 2, PAD + T], F32, temps)
            p_raw = sb("p_raw", [P, NP_, T], F32, temps)
            lru_act = sb("lru_act", [P, 4, T], F32, temps)
            lru_a = sb("lru_a", [P, 2, T], F32, temps)
            decay = sb("decay", [P, NI], F32, temps)
            half_b = sb("half_b", [P, 2, NI], F32, temps)
            tiny = sb("tiny", [P, 4, NI], F32, temps)
        tab = sb("tab", [P, N_TABLES])
        acc_kv = sb("acc_kv", [P, T])
        rstd_kv = sb("rstd_kv", [P, T])
        rope_cos, rope_sin = sb("rope_cos", [P, T]), sb("rope_sin", [P, T])
        with ExitStack() as block1:
            inner = sb("inner", [P, NI, 2 * T], F32R, block1)
            wide = sb("wide", [P, NI, T], F32, block1)
        with ExitStack() as overlay:
            gated = sb("gated", [P, ND, T], F32, overlay)
        with ExitStack() as overlay:
            sb("inner_again", [P, NI, 2 * T], F32R, overlay)
            win = sb("win", [P, 6, PAD + T], F32, overlay)
            inv_count = sb("inv_count", [P, 4, T], F32, overlay)
        o_buf, x_buf = wide[:, 0:ND, :], wide[:, ND:NI, :]
        with ExitStack() as overlay:
            y_abc = sb("y_abc", [P, 24, 2 * T], F32R, overlay)
            scr = sb("scr", [P, 8192], F32, overlay)
        with ExitStack() as overlay:
            latent = sb("latent", [P, 8, 2 * T], F32R, overlay)
            scr2 = sb("scr2", [P, 8192], F32, overlay)
            merged = sb("merged", [P, ND, 2 * T], F32R, overlay)
        with ExitStack() as overlay:
            pos_int = sb("pos_int", [P, T], mybir.dt.int32, overlay)

        def view(buf, at, *shape):
            n = int(np.prod(shape))
            part = buf[:, at:at + n]
            if len(shape) == 2:
                part = part.rearrange("p (a b) -> p a b", b=shape[1])
            return part

        gqk = view(scr2, 0, 8, T)
        b_cum = view(scr2, 2048, 4, T)
        g_x, g_e, g_t = (view(scr2, a, 4, T) for a in (3072, 4096, 5120))
        g_s2 = view(scr2, 6144, 4, T)
        g_d, g_q, g_k = g_x, g_e, g_t
        g_m = [view(scr2, 6144, LEVELS, P), view(scr2, 7168, LEVELS, P)]
        g_v = view(scr, 0, 2, 1024)
        g_o = view(scr, 2048, 8, T)
        v_raw = view(scr, 4096, 8, T)
        wa2 = view(scr, 6144, 512)
        g_a = view(scr, 6656, 3, P)
        g_sq = view(scr, 7040, 2, T)
        g_rstd = view(scr, 7552, T)
        ka = view(scr, 7808, T)
        q_buf = view(scr2, 0, 12, T)
        k_buf = view(scr2, 3072, 8, T)
        kr = view(scr2, 5120, 2, T)
        r1, r2 = view(scr2, 5632, 2, T), view(scr2, 6144, 2, T)
        qm = view(scr2, 6656, 2, T)
        k_sq, k_rstd = view(scr2, 7168, T), view(scr2, 7424, T)
        q_var, q_rstd, q_scale = (view(scr2, a, 16) for a in (7680, 7696, 7712))
        s_max, s_bias, s_sum, s_inv = (view(scr2, a, 2) for a in (7728, 7730, 7732, 7734))
        kr_sq = view(scr2, 7936, T)
        a_v = view(scr, 0, 2, 1024)
        q_sq = view(scr, 6144, 6, T)
        probs, probs_t, att_s = (view(scr, a, 384) for a in (6144, 6528, 6912))
        s_v = view(scr, 0, 8, T)
        s_vt = view(scr, 2048, 2, 1024)
        s_mix = view(scr, 4096, 8, T)
        w_st = view(scr, 6144, S_GROUPS, P)
        s_col, s_rstd = view(scr, 7168, 2), view(scr, 7170, 2)
        b_st = view(scr2, 0, S_GROUPS, P)

        banks = ctx.enter_context(nc.psum_tensor("banks", [P, BANKS, 2 * T], F32))
        ms_bank = ctx.enter_context(nc.psum_tensor("ms_bank", [P, 2 * T], F32))
        pm = ctx.enter_context(nc.psum_tensor("pm", [P, 3, 2 * T], F32))

        raw_in = [sem(f"raw_in{s}") for s in range(SLOTS)]
        hi_done, lo_done, unit_used = sem("hi_done"), sem("lo_done"), sem("unit_used")
        small_ready, bank_free = sem("small_ready"), sem("bank_free")
        val_ready, act_ready, res_ready = sem("val_ready"), sem("act_ready"), sem("res_ready")
        pool_done, tile_split = sem("pool_done"), sem("tile_split")
        consts_in, consts_ready, x_loaded, x_saved = (sem("consts_in"), sem("consts_ready"),
                                                      sem("x_loaded"), sem("x_saved"))
        p_loaded, p_hi, p_ready = sem("p_loaded"), sem("p_hi"), sem("p_ready")
        x_updated, x_hi, x_sq, xs_ready = sem("x_updated"), sem("x_hi"), sem("x_sq"), sem("xs_ready")
        acc_ready, ms_ready, root_ready, rstd_ready = (sem("acc_ready"), sem("ms_ready"),
                                                      sem("root_ready"), sem("rstd_ready"))
        acc_zero, sq_added = sem("acc_zero"), sem("sq_added")
        lru_root, lru_sig, lru_p, lru_at, lru_m, lru_b, lru_y = (
            sem("lru_root"), sem("lru_sig"), sem("lru_p"), sem("lru_at"), sem("lru_m"), sem("lru_b"),
            sem("lru_y"))
        decay_e, out_done = sem("decay_e"), sem("out_done")
        tables_in, small_in, pos_ready, rope_arg, rope_done = (
            sem("tables_in"), sem("small_in"), sem("pos_ready"), sem("rope_arg"), sem("rope_done"))
        inner_ready = sem("inner_ready")
        turned, turn_read = sem("turned"), sem("turn_read")
        gla_logit, gla_arg, gla_exp, gla_cum = (sem("gla_logit"), sem("gla_arg"), sem("gla_exp"),
                                                sem("gla_cum"))
        gla_scores_read = sem("gla_scores_read")
        gla_diff, gla_decay, gla_qk, gla_scores, gla_mixed, gla_out, gla_sq, gla_normed = (
            sem("gla_diff"), sem("gla_decay"), sem("gla_qk"), sem("gla_scores"), sem("gla_mixed"),
            sem("gla_out"), sem("gla_sq"), sem("gla_normed"))
        att_qsq, att_rsq, att_qms, att_qvar, att_qrstd, att_rep, att_roped = (
            sem("att_qsq"), sem("att_rsq"), sem("att_qms"), sem("att_qvar"), sem("att_qrstd"),
            sem("att_rep"), sem("att_roped"))
        att_ksq, att_qm, att_scores, att_max, att_exp, att_probs, att_turned, att_pt, att_o, att_done = (
            sem("att_ksq"), sem("att_qm"), sem("att_scores"), sem("att_max"), sem("att_exp"),
            sem("att_probs"), sem("att_turned"), sem("att_pt"), sem("att_o"), sem("att_done"))
        sgu_ms, sgu_var, sgu_rstd, sgu_w, sgu_mix, sgu_read, sgu_in = (
            sem("sgu_ms"), sem("sgu_var"), sem("sgu_rstd"), sem("sgu_w"), sem("sgu_mix"),
            sem("sgu_read"), sem("sgu_in"))
        act_chain = Chain(sem("act_chain"))
        dve_chain, pool_chain = Chain(sem("dve_chain")), Chain(sem("pool_chain"))

        def col(name, m, n=1):
            c = COLUMN[name]
            return chan[:, bass.ds(m + c, n)] if not isinstance(m, int) else chan[:, c + m:c + m + n]

        from_xs = lambda turn, k: xs[:, k, :]
        from_inner = lambda turn, k: inner[:, k, :]
        stages = []

        def stage(name, products, turns, signals, count=None, unroll=False):
            s = Stage(name, products, turns)
            s.layer, s.unroll = layer, unroll
            s.counts = {}
            s.signals, s.count = signals, count or turns * len(products)
            stages.append(s)

        for layer in range(2):
            if layer == 0:
                stage("window", [Product(ND, from_xs) for _ in range(4)], NI // 4, "v p")
                stage("pooled", [Product(8, lambda turn, k: inner[:, turn * 8 + k, :])
                                 for _ in range(8)], NI // 8, "")
                stage("silu", [Product(ND, from_xs) for _ in range(4)], NI // 4, "v t q p")
            else:
                stage("conv", [Product(ND, from_xs) for _ in range(4)], NI // 4, "q p")
                lru = []
                for h in range(4):
                    lru += [Product(2, lambda turn, k, h=h: inner[:, turn * 8 + 2 * h + k, :])
                            for _ in range(4)] + [Product(ND, from_xs) for _ in range(2)]
                stage("lru", lru, HEADS // 4, "v t q p", count=NI)
            stage("squared", [Product(NI, from_inner) for _ in range(4)], ND // 4, "p")
            stage("plain", [Product(NP_, from_xs) for _ in range(16)], 1, "")
            stage("gate", [Product(ND, from_xs) for _ in range(4)], ND // 4, "v t q p")
        for layer in (2, 3):
            four = lambda: [Product(ND, from_xs) for _ in range(4)]
            stage("latent", four(), 2, "v t q p", unroll=True)
            stage("rope_k", [Product(ND, from_xs)], 1, "v", unroll=True)
            stage("gqk", four(), 2, "v")
            stage("gv", four(), 2, "v")
            stage("uq", [Product(4, lambda turn, k: latent[:, k, :]) for _ in range(12)], 1, "v",
                  unroll=True)
            stage("ukv", [Product(4, lambda turn, k: latent[:, 4 + k, :]) for _ in range(16)], 1, "v",
                  unroll=True)
            stage("za", four(), 2, "v t q p")
            stage("zc", four(), 2, "v t q p")
            stage("vb", four(), 2, "v t q p", unroll=True)
            stage("ub", four(), 2, "v t q", unroll=True)
            stage("zb", four(), 2, "v t q p")
            mix = []
            for _ in range(4):
                for branch in range(3):
                    mix.append(Product(ND, from_xs))
                    mix.append(Product(8, lambda turn, k, b=branch: y_abc[:, 8 * b + k, :]))
            stage("mix", mix, ND // 4, "v t q p")
            stages[-1].counts = {"v": 3 * ND, "t": 3 * ND, "q": ND, "p": ND}
            stage("wo", [Product(ND, lambda turn, k: merged[:, k, :]) for _ in range(4)], ND // 4, "q")
        COUNTED = {"v": val_ready, "t": act_ready, "q": res_ready, "p": pool_done}
        unit0 = bank0 = 0
        base = dict.fromkeys(COUNTED, 0)
        for s in stages:
            s.unit0, s.bank0, s.base = unit0, bank0, dict(base)
            unit0 += s.turns * s.units
            bank0 += s.turns * s.width
            for c in s.signals.split():
                base[c] += s.counts.get(c, s.count)
            s.end = dict(base)
            s.last_unit = unit0
        n_units = unit0
        assert n_units == weights.shape[0], (n_units, weights.shape)
        norms = {}
        for l in range(2):
            for which in ("enter", "out", "ple", "gate"):
                norms[l, which] = len(norms)
        for l in (2, 3):
            for which in (["enter", "cq", "ckv"] + [f"gla{h}" for h in range(G_HEADS)]
                          + [f"k{h}" for h in range(A_HEADS)]):
                norms[l, which] = len(norms)
        ends = {(s.layer, s.name): s.end for s in stages}

        block = ctx.enter_context(nc.Block())

        @block.sync
        def _(sp):
            def load(n, slot):
                if isinstance(n, int) and n >= n_units:
                    return
                wait(sp, lo_done, n - SLOTS + 1)
                sp.dma_start(raw[:, slot, :], weights[n]).then_inc(raw_in[slot], 16)

            sp.dma_start(chan[:], channels).then_inc(consts_in, 16)
            for n in range(LOOKAHEAD):
                load(n, n % SLOTS)

            for s in stages:
                def turn(i):
                    for u in range(s.units):
                        load(i * s.units + (s.unit0 + u + LOOKAHEAD),
                             (s.unit0 + u + LOOKAHEAD) % SLOTS)
                static = 1 if s is stages[-1] else 0
                if s.turns - static > 1:
                    with sp.Fori(0, s.turns - static) as i:
                        turn(i)
                    if static:
                        turn(s.turns - 1)
                else:
                    for i in range(s.turns):
                        turn(i)

        def run_stage(eng, s, turn, per=None, chain=None):
            turn(0)
            if s.unroll:
                for i in range(1, s.turns):
                    turn(i)
                return
            last = 1 if s is stages[-1] else 0
            n = s.turns - 1 - last
            if n > 0:
                with eng.Fori(1, n + 1) as i:
                    if chain is not None:
                        with chain.loop(i - 1, n, per):
                            turn(i)
                    else:
                        turn(i)
            if last:
                turn(s.turns - 1)

        def unit_of(s, i, u):
            return i * s.units + (s.unit0 + u)

        def bank_of(s, i, j):
            return i * s.width + (s.bank0 + j)

        def before(s, i, j):
            return (i, j - 1) if j else (i - 1, s.width - 1)

        @block.tensor
        def _(pe):
            def products(s, i, ready=None, after_first=None):
                tile = 0
                for j, p in enumerate(s.products):
                    bank = banks[:, (s.bank0 + j) % BANKS, :]
                    wait(pe, bank_free, bank_of(s, i, j) - BANKS + 1)
                    for k in range(p.depth):
                        u, c = divmod(p.first_tile + k, UNIT_TILES)
                        slot = (s.unit0 + u) % SLOTS
                        if c == 0:
                            pe.wait_ge(lo_done, unit_of(s, i, u) + 1)
                        if ready is not None and j == 0:
                            ready(k)
                        w = slice(c * P, (c + 1) * P)
                        x = p.operand(i, k)
                        nc.tensor.matmul(bank, w_hi[:, slot, w], x, start=(k == 0), stop=False)
                        ins = nc.tensor.matmul(bank[:, T:2 * T], w_lo[:, slot, w], x[:, 0:T],
                                               start=False, stop=(k == p.depth - 1))
                        if c == UNIT_TILES - 1:
                            ins.then_inc(unit_used, 1)
                    if j == 0 and after_first is not None:
                        after_first()

            def mean_square(l, which, source, weights_=None):
                q = norms[l, which]
                if q:
                    pe.wait_ge(root_ready, q)
                for j, a in enumerate(source):
                    ins = nc.tensor.matmul(ms_bank[:, 0:T], (weights_ or [mean_d[:, :]] * 9)[j], a,
                                           start=(j == 0), stop=(j == len(source) - 1))
                ins.then_inc(ms_ready, 1)

            def mean_square_x(l, which, feed_):
                pe.wait_ge(sq_added, feed_ * 4 + 4)
                mean_square(l, which, act4)

            def turn_tiles(c, use, source):
                for r in range(4):
                    R = (c * 3 + use) * 4 + r
                    wait(pe, turn_read, R - 1)
                    for t in range(4):
                        ins = nc.tensor.transpose(
                            pm[:, r % 2, t * P:(t + 1) * P],
                            source[:, (r % 2) * 4 + t, (r // 2) * P:(r // 2 + 1) * P], tab[:, TABLE["ident"]])
                    ins.then_inc(turned, 1)

            def gla_logits(c):
                pe.wait_ge(small_in, 16 * (c + 1))
                pe.wait_ge(turn_read, c * 12 + 4)
                for h in range(G_HEADS):
                    ins = nc.tensor.matmul(pm[:, h // 2, (h % 2) * T:(h % 2 + 1) * T],
                                           wa2[:, h * P:(h + 1) * P], ka, start=True, stop=True)
                ins.then_inc(gla_logit, 1)

            def gla_head(c, h):
                g = c * G_HEADS + h
                for half in range(2):
                    pe.wait_ge(gla_qk, 2 * g + half + 1)
                    if half == 0 and g:
                        pe.wait_ge(gla_normed, g)
                    for chunk in range(2):
                        for t in range(4):
                            span = slice(chunk * P, (chunk + 1) * P)
                            if half and t == 3:
                                k_, q_ = gqk[:, 4 + h, span], gqk[:, h, span]
                            else:
                                k_, q_ = g_k[:, t, span], g_q[:, t, span]
                            if half and not t:
                                pe.wait_ge(gla_scores_read, 2 * g + 1)
                            ins = nc.tensor.matmul(pm[:, chunk, t * P:(t + 1) * P], k_, q_,
                                                   start=True, stop=True)
                    if half:
                        ins = nc.tensor.matmul(pm[:, 2, 0:P], g_k[:, 3, 0:P], g_q[:, 3, P:2 * P],
                                               start=True, stop=True)
                    ins.then_inc(gla_scores, 1)
                pe.wait_ge(gla_mixed, g + 1)
                for j in range(2):
                    v0, v1 = (g_v[:, b, h * T + j * P:h * T + (j + 1) * P] for b in range(2))
                    nc.tensor.matmul(pm[:, 2, j * T:j * T + P], v0, g_a[:, 0, :], start=True, stop=True)
                    nc.tensor.matmul(pm[:, 2, j * T + P:(j + 1) * T], v1, g_a[:, 1, :], start=True,
                                     stop=False)
                    ins = nc.tensor.matmul(pm[:, 2, j * T + P:(j + 1) * T], v0, g_a[:, 2, :],
                                           start=False, stop=True)
                ins.then_inc(gla_out, 1)
                pe.wait_ge(gla_sq, g + 1)
                mean_square(c + 2, f"gla{h}", [g_sq[:, 0, :], g_sq[:, 1, :]])

            def attention_start(c):
                pe.wait_ge(att_rsq, c + 1)
                pe.wait_ge(gla_normed, (c + 1) * G_HEADS)
                for half in range(2):
                    pe.wait_ge(att_qsq, 2 * c + half + 1)
                    for tb in range(2):
                        tok = slice(tb * P, (tb + 1) * P)
                        at = tb * 8 + half * 4
                        nc.tensor.matmul(pm[:, 2, at:at + 4], q_sq[:, 4 + half, tok], tab[:, TABLE["sel"]],
                                         start=(half == tb == 0), stop=False, skip_group_check=True)
                        for h in range(4):
                            ins = nc.tensor.matmul(pm[:, 2, at + h:at + h + 1], q_sq[:, h, tok],
                                                   ones_col, start=False,
                                                   stop=(half == tb == 1 and h == 3),
                                                   skip_group_check=True)
                    ins.then_inc(att_qms, 1)
                pe.wait_ge(turn_read, c * 12 + 8)
                nc.tensor.matmul(pm[:, 0, 0:T], tab[:, TABLE["rep1"]], ka, start=True, stop=True)
                nc.tensor.matmul(pm[:, 0, T:2 * T], tab[:, TABLE["rep2"]], ka, start=True, stop=True)\
                    .then_inc(att_rep, 1)

            def attention_head(c, h):
                g, grp = c * A_HEADS + h, h // 4
                pe.wait_ge(att_ksq, g + 1)
                pe.wait_ge(att_roped, c + 1)
                mean_square(c + 2, f"k{h}", [k_sq, kr_sq], [mean_d[:, :], tab[:, TABLE["rope_rows"]]])
                pe.wait_ge(att_qm, g + 1)
                for tb in range(2):
                    keys = slice(0, (tb + 1) * P)
                    o_ = pm[:, 0, 0:P] if tb == 0 else pm[:, 0, P:3 * P]
                    tok = slice(tb * P, (tb + 1) * P)
                    nc.tensor.matmul(o_, q_buf[:, h, tok], k_buf[:, h, keys], start=True, stop=False)
                    nc.tensor.matmul(o_, qm[:, 0, tok], kr[:, 0, keys], start=False, stop=False)
                    ins = nc.tensor.matmul(o_, qm[:, 1, tok], kr[:, 1, keys], start=False, stop=True)
                ins.then_inc(att_scores, 1)
                pe.wait_ge(att_probs, g + 1)
                for t in range(3):
                    ins = nc.tensor.transpose(pm[:, 1, t * P:(t + 1) * P], probs[:, t * P:(t + 1) * P],
                                              tab[:, TABLE["ident"]])
                ins.then_inc(att_turned, 1)
                pe.wait_ge(att_pt, g + 1)
                wait(pe, att_done, g)
                v0, v1 = (a_v[:, b, h * P:(h + 1) * P] for b in range(2))
                nc.tensor.matmul(pm[:, 2, 0:P], v0, probs_t[:, 0:P], start=True, stop=True)
                nc.tensor.matmul(pm[:, 2, P:T], v0, probs_t[:, P:2 * P], start=True, stop=False)
                nc.tensor.matmul(pm[:, 2, P:T], v1, probs_t[:, 2 * P:3 * P], start=False, stop=True)\
                    .then_inc(att_o, 1)

            def spatial_gate(c):
                pe.wait_ge(pool_done, ends[c + 2, "vb"]["p"])
                pe.wait_ge(att_done, (c + 1) * A_HEADS)
                for tb in range(2):
                    ins = nc.tensor.matmul(pm[:, 2, tb:tb + 1], acc[:, tb * P:(tb + 1) * P],
                                           mean_d[:, 0:1], start=(tb == 0), stop=(tb == 1),
                                           skip_group_check=True)
                ins.then_inc(sgu_ms, 1)
                turn_tiles(c, 2, s_v)
                pe.wait_ge(sgu_w, c + 1)
                pe.wait_ge(turn_read, c * 12 + 12)
                for g in range(S_GROUPS):
                    r = c * S_GROUPS + g
                    if g >= 2:
                        pe.wait_ge(sgu_read, r - 1)
                    for chunk in range(2):
                        ins = nc.tensor.matmul(pm[:, g % 2, chunk * P:(chunk + 1) * P],
                                               s_vt[:, chunk, g * P:(g + 1) * P], w_st[:, g, :],
                                               start=True, stop=True)
                    ins.then_inc(sgu_mix, 1)

            act4 = [act[:, j, :] for j in range(4)]
            pe.wait_ge(consts_ready, 1)
            feeds = 0
            for n, s in enumerate(stages):
                l = s.layer
                ready = hook = None
                if s.name in ("window", "conv", "latent"):
                    ready = lambda k, f=feeds: pe.wait_ge(xs_ready, f * ND + k + 1)
                    hook = lambda f=feeds: mean_square_x(l, "enter", f)
                    feeds += 1
                elif s.name == "gate":
                    ready = lambda k, f=feeds: pe.wait_ge(xs_ready, f * ND + k + 1)
                    hook = lambda f=feeds: mean_square_x(l, "ple", f)
                    feeds += 1
                elif s.name == "squared":
                    ready = lambda k, b=stages[n - 1].base["p"]: pe.wait_ge(pool_done, b + k + 1)
                elif s.name == "plain":
                    ready = lambda k: pe.wait_ge(p_ready, l * NP_ + k + 1)
                elif s.name == "wo":
                    ready = lambda k, b=stages[n - 1].base["p"]: pe.wait_ge(pool_done, b + k + 1)
                if s.name in ("lru", "mix"):
                    pe.wait_ge(pool_done, s.base["p"])
                if s.name in ("uq", "ukv"):
                    pe.wait_ge(res_ready, ends[l, "latent"]["q"])

                def turn(i):
                    if s.name == "pooled":
                        pe.wait_ge(tile_split, i * 8 + 8)
                    static = isinstance(i, int) and i == 0
                    products(s, i, ready if static else None, hook if static else None)
                run_stage(pe, s, turn)
                if s.name in ("plain", "gate"):
                    pe.wait_ge(pool_done, s.end["p"])
                    mean_square(l, "out" if s.name == "plain" else "gate", [acc[:, :]])
                if s.name == "rope_k":
                    pe.wait_ge(pool_done, s.base["p"])
                    mean_square(l, "cq", [acc[:, :]])
                    mean_square(l, "ckv", [acc_kv[:, :]])
                if s.name == "gv":
                    pe.wait_ge(val_ready, s.end["v"])
                    pe.wait_ge(tables_in, 16)
                    wait(pe, sgu_read, (l - 2) * S_GROUPS)
                    turn_tiles(l - 2, 0, v_raw)
                    gla_logits(l - 2)
                    for h in range(G_HEADS):
                        gla_head(l - 2, h)
                if s.name == "ukv":
                    pe.wait_ge(val_ready, s.end["v"])
                    turn_tiles(l - 2, 1, v_raw)
                    attention_start(l - 2)
                    for h in range(A_HEADS):
                        attention_head(l - 2, h)
                if s.name == "vb":
                    spatial_gate(l - 2)

        @block.scalar
        def _(sc):
            def split_hi(n, slot):
                if isinstance(n, int) and n >= n_units:
                    return
                sc.wait_ge(raw_in[slot], (n - slot) * 4 + 16)
                wait(sc, unit_used, n - SLOTS + 1)
                nc.scalar.activation(w_hi[:, slot, :], raw[:, slot, :], ACT.Copy).then_inc(hi_done, 1)

            def read_small(s, i, j):
                b = (s.bank0 + j) % BANKS
                sc.wait_ge(unit_used, unit_of(s, i, s.products[j].last_unit) + 1)
                wait(sc, bank_free, bank_of(s, i, j) - 1)
                nc.scalar.activation(small[:, b % 2, :], banks[:, b, T:2 * T], ACT.Copy)\
                    .then_inc(small_ready, 1)

            def feed(f, gain, first):
                for b in range(4):
                    if first:
                        if b == 0:
                            sc.wait_ge(x_loaded, 16)
                            sc.wait_ge(consts_in, 16)
                    elif f == 5:
                        sc.wait_ge(res_ready, ends[2, "wo"]["q"])
                    else:
                        sc.wait_ge(x_updated, (f - 1) * 4 + b + 1)
                    for k in range(4 * b, 4 * b + 4):
                        nc.scalar.activation(xs[:, k, 0:T], x_buf[:, k, :], ACT.Copy,
                                             scale=col(gain, k)).then_inc(x_hi, 1)
                    wait(sc, sq_added, f * 4 + b)
                    nc.scalar.activation(val[:, :, :], x_buf[:, 4 * b:4 * b + 4, :], ACT.Square)\
                        .then_inc(x_sq, 1)

            def root(l, which, width=D):
                q = norms[l, which]
                sc.wait_ge(ms_ready, q + 1)
                wait(sc, rstd_ready, q)
                nc.scalar.activation(rms[:], ms_bank[:, 0:T], ACT.Sqrt, scale=D / width,
                                     bias=eps_col).then_inc(root_ready, 1)

            def rope_tables():
                sc.wait_ge(rope_arg, 1)
                nc.scalar.activation(rope_sin[:], sq[:], ACT.Sin).then_inc(rope_done, 1)
                nc.scalar.activation(rope_cos[:], acc_kv[:], ACT.Sin).then_inc(rope_done, 1)

            def read_turned(c, use, dest, scale=None):
                for r in range(4):
                    R = (c * 3 + use) * 4 + r
                    sc.wait_ge(turned, R + 1)
                    d = dest[:, r // 2, (r % 2) * 512:(r % 2 + 1) * 512]
                    if scale is None:
                        ins = nc.scalar.activation(d, pm[:, r % 2, :], ACT.Copy)
                    else:
                        ins = nc.scalar.activation(d, pm[:, r % 2, :], ACT.Copy,
                                                   scale=scale[:, r // 2:r // 2 + 1])
                    ins.then_inc(turn_read, 1)

            def gla(c):
                read_turned(c, 0, g_v)
                sc.wait_ge(gla_arg, c + 1)
                act_chain.link(sc, nc.scalar.activation(g_e, g_x, ACT.Abs))
                nc.scalar.activation(g_e, g_e, ACT.Exp, scale=-1.0).then_inc(gla_exp, 1)
                for h in range(G_HEADS):
                    g = c * G_HEADS + h
                    for half in range(2):
                        sc.wait_ge(gla_diff, 2 * g + half + 1)
                        act_chain.link(sc, nc.scalar.activation(g_d, g_d, ACT.Abs))
                        nc.scalar.activation(g_d, g_d, ACT.Exp, scale=-1.0).then_inc(gla_decay, 1)
                    sc.wait_ge(gla_out, g + 1)
                    nc.scalar.activation(g_sq.rearrange("p a b -> p (a b)"), pm[:, 2, :], ACT.Square)\
                        .then_inc(gla_sq, 1)
                    root(c + 2, f"gla{h}", 2 * P)

            def attention(c):
                read_turned(c, 1, a_v)
                for half in range(2):
                    wait(sc, att_qms, 2 * c + half)
                    nc.scalar.activation(q_sq[:, 0:4, :], q_buf[:, 4 * half:4 * half + 4, :], ACT.Square)\
                        .then_inc(att_qsq, 1)
                for h in range(A_HEADS):
                    g = c * A_HEADS + h
                    wait(sc, att_scores, g)
                    nc.scalar.activation(k_sq, k_buf[:, h, :], ACT.Square).then_inc(att_ksq, 1)
                    root(c + 2, f"k{h}", QK)
                    sc.wait_ge(att_max, g + 1)
                    for tb in range(2):
                        span = slice(0, P) if tb == 0 else slice(P, 3 * P)
                        nc.scalar.activation(probs[:, span], att_s[:, span], ACT.Exp,
                                             scale=q_scale[:, tb * 8 + h:tb * 8 + h + 1],
                                             bias=s_bias[:, tb:tb + 1],
                                             accum_out=s_sum[:, tb:tb + 1]).then_inc(att_exp, 1)
                    sc.wait_ge(att_turned, g + 1)
                    nc.scalar.activation(probs_t, pm[:, 1, 0:3 * P], ACT.Copy).then_inc(att_pt, 1)
                    sc.wait_ge(att_o, g + 1)
                    nc.scalar.activation(q_buf[:, h, :], pm[:, 2, 0:T], ACT.Copy).then_inc(att_done, 1)

            def spatial_gate(c):
                sc.wait_ge(sgu_rstd, c + 1)
                read_turned(c, 2, s_vt, s_rstd)

            sc.dma_start(x_buf, x_in).then_inc(x_loaded, 16)
            sc.dma_start(inv_count[:], inv_counts).then_inc(consts_in, 16)
            for n in range(LOOKAHEAD):
                split_hi(n, n % SLOTS)
            sc.wait_ge(consts_in, 32)
            nc.scalar.activation(tiny[:, 1, :], col("lru_L", 0, NI), ACT.Abs).then_inc(decay_e, 1)
            sc.wait_ge(decay_e, 1)
            nc.scalar.activation(tiny[:, 0, :], tiny[:, 1, :], ACT.Exp, scale=-1.0).then_inc(decay_e, 1)
            feeds = gelus = 0
            for n, s in enumerate(stages):
                l = s.layer
                if s.name in ("window", "conv"):
                    if l:
                        root(0, "gate")
                    feed(feeds, f"g_pre{l}", feeds == 0)
                    if feeds:
                        sc.dma_start(x_scratch, x_buf).then_inc(x_saved, 16)
                    feeds += 1
                if s.name == "squared":
                    sc.wait_ge(res_ready, s.base["q"])
                    sc.dma_start(x_buf, x_scratch if l else x_in).then_inc(x_loaded, 16)
                    sc.dma_start(p_raw[:], p_in[l]).then_inc(p_loaded, 16)
                    sc.wait_ge(p_loaded, 16 * (l + 1))
                    sc.wait_ge(unit_used, s.unit0)
                    nc.scalar.activation(xs[:, 0:NP_, 0:T], p_raw[:], ACT.Copy).then_inc(p_hi, 1)
                if s.name == "gate":
                    root(l, "out")
                    feed(feeds, f"g_ple_in{l}", False)
                    feeds += 1
                if s.name == "latent":
                    if l == 2:
                        root(1, "gate")
                    feed(feeds, f"norm_g{l - 2}", False)
                    feeds += 1
                    if l == 2:
                        sc.dma_start(tab[:], tables).then_inc(tables_in, 16)
                        sc.dma_start(pos_int[:], positions).then_inc(pos_ready, 16)
                        rope_tables()
                if s.name == "rope_k":
                    sc.wait_ge(unit_used, s.unit0)
                    sc.dma_start(wa2, w_a2[l - 2]).then_inc(small_in, 16)
                if s.name == "vb":
                    sc.wait_ge(res_ready, s.base["q"])
                    sc.dma_start(w_st, w_s[l - 2]).then_inc(sgu_in, 16)
                    sc.dma_start(b_st, b_s[l - 2]).then_inc(sgu_in, 16)

                def head(i, h):
                    m = i * 8 + 2 * h
                    t = i * 4 + h
                    for j in range(4):
                        sc.wait_ge(bank_free, bank_of(s, i, 6 * h + j) + 1)
                        if j == 0:
                            wait(sc, lru_y, t)
                        nc.scalar.activation(lru_act[:, j, :], val[:, j, :], ACT.Tanh, scale=0.5,
                                             bias=half_b[:, j // 2, bass.ds(m + j % 2, 1)]
                                             if not isinstance(m, int) else
                                             half_b[:, j // 2, m + j % 2:m + j % 2 + 1])\
                            .then_inc(lru_sig, 1)

                def head_decay(i, h):
                    t = i * 4 + h
                    sc.wait_ge(lru_p, t + 1)
                    nc.scalar.activation(lru_a[:, :, :], val[:, 0:2, :], ACT.Exp, scale=-1.0)\
                        .then_inc(lru_at, 1)
                    nc.scalar.activation(lru_act[:, 0:2, :], val[:, 0:2, :], ACT.Tanh)\
                        .then_inc(lru_at, 1)

                def head_root(i, h):
                    t = i * 4 + h
                    sc.wait_ge(lru_m, t + 1)
                    nc.scalar.activation(lru_act[:, 0:2, :], lru_act[:, 0:2, :], ACT.Sqrt)\
                        .then_inc(lru_root, 1)

                def turn(i):
                    for u in range(s.units):
                        n_ = s.unit0 + u + LOOKAHEAD
                        split_hi(i * s.units + n_, n_ % SLOTS)
                        for j, p in enumerate(s.products):
                            if p.last_unit != u:
                                continue
                            if s.name == "lru" and j % 6 == 4:
                                head_root(i, j // 6)
                            read_small(s, i, j)
                            if (s.name in ("window", "conv", "latent", "gate")
                                    and isinstance(i, int) and i == j == 0):
                                root(l, "ple" if s.name == "gate" else "enter")
                            m = i * s.width + j
                            if s.name == "latent":
                                sc.wait_ge(val_ready, m + s.base["v"] + 1)
                                nc.scalar.activation(latent[:, m, 0:T], val[:, j % 4, :], ACT.Copy,
                                                     scale=col(("cq_g%d" if m < 4 else "ckv_g%d")
                                                               % (l - 2), m % 4)).then_inc(act_ready, 1)
                            if s.name in ("vb", "ub") and m:
                                gelu_tanh(m - 1)
                            if s.name == "mix" and j % 2 == 0:
                                pair = i * (s.width // 2) + j // 2
                                slot = (j // 2) % 2
                                sc.wait_ge(val_ready, pair + (s.base["v"] + 1))
                                nc.scalar.activation(act[:, slot, :], val[:, 2 * slot, :], ACT.Tanh,
                                                     scale=0.5).then_inc(act_ready, 1)
                            if s.name in ("silu", "gate", "za", "zc", "zb"):
                                sc.wait_ge(val_ready, m + (s.base["v"] + 1))
                                wait(sc, pool_done, m + (s.base["p"] - 3))
                                nc.scalar.activation(act[:, j % 4, :], val[:, j % 4, :], ACT.Tanh,
                                                     scale=0.5).then_inc(act_ready, 1)
                            if s.name == "lru":
                                h, q = divmod(j, 6)
                                if q == 3:
                                    head(i, h)
                                    head_decay(i, h)
                                if q >= 4:
                                    z = i * 8 + 2 * h + (q - 4)
                                    sc.wait_ge(val_ready, z + (s.base["v"] + 1))
                                    wait(sc, pool_done, z + (s.base["p"] - 1))
                                    nc.scalar.activation(act[:, q - 4, :], val[:, q - 2, :], ACT.Tanh,
                                                         scale=0.5).then_inc(act_ready, 1)

                def gelu_tanh(m):
                    sc.wait_ge(inner_ready, gelus * 8 + m + 1)
                    a = act[:, m % 4, :]
                    nc.scalar.activation(a, a, ACT.Tanh, scale=GELU_A).then_inc(act_ready, 1)

                run_stage(sc, s, turn)
                if s.name in ("vb", "ub"):
                    gelu_tanh(7)
                    gelus += 1
                if s.name == "rope_k":
                    root(l, "cq", RANK)
                    root(l, "ckv", RANK)
                if s.name == "gv":
                    gla(l - 2)
                if s.name == "ukv":
                    attention(l - 2)
                if s.name == "vb":
                    spatial_gate(l - 2)
            sc.wait_ge(res_ready, stages[-1].end["q"])
            sc.dma_start(out, x_buf).then_inc(out_done, 16)
            sc.wait_ge(out_done, 16)

        @block.vector
        def _(ve):
            link = lambda ins: dve_chain.link(ve, ins)

            def split_lo(n, slot):
                if isinstance(n, int) and n >= n_units:
                    return
                ve.wait_ge(hi_done, n + 1)
                nc.vector.tensor_tensor(w_lo[:, slot, :], raw[:, slot, :], w_hi[:, slot, :].bitcast(F32),
                                        ALU.subtract).then_inc(lo_done, 1)

            def read_bank(s, i, j, out_):
                b = (s.bank0 + j) % BANKS
                ve.wait_ge(small_ready, bank_of(s, i, j) + 1)
                ins = nc.vector.tensor_tensor(out_, banks[:, b, 0:T], small[:, b % 2, :], ALU.add)
                ins.then_inc(bank_free, 1)
                ve.wait_ge(bank_free, bank_of(s, i, j) + 1)
                return ins

            def norm(l, which, dest):
                q = norms[l, which]
                ve.wait_ge(root_ready, q + 1)
                nc.vector.reciprocal(dest[:, 0:T], rms[:]).then_inc(rstd_ready, 1)
                ve.wait_ge(rstd_ready, q + 1)

            def feed(f, gain, residual):
                if residual is not None:
                    source, res_gain, l, which = residual
                    norm(l, which, rstd_r)

                def lows(b):
                    for k in range(4 * b, 4 * b + 4):
                        ve.wait_ge(x_hi, f * ND + k + 1)
                        nc.vector.scalar_tensor_tensor(
                            out=xs[:, k, T:2 * T], in0=x_buf[:, k, :], scalar=col(gain, k),
                            in1=xs[:, k, 0:T].bitcast(F32), op0=ALU.mult, op1=ALU.subtract)\
                            .then_inc(xs_ready, 1)
                for b in range(4):
                    if residual is not None:
                        r4 = source[:, 4 * b:4 * b + 4, :]
                        link(nc.vector.tensor_tensor(
                            r4, r4, rstd_r[:, None, :].broadcast_to([P, 4, T]), ALU.mult))
                        for k in range(4 * b, 4 * b + 4):
                            ins = nc.vector.scalar_tensor_tensor(
                                out=x_buf[:, k, :], in0=source[:, k, :], scalar=col(res_gain, k),
                                in1=x_buf[:, k, :], op0=ALU.mult, op1=ALU.add)
                        ins.then_inc(x_updated, 1)
                    if gain is not None and b:
                        lows(b - 1)
                if gain is not None:
                    lows(3)

            def log1p_over_2(s_, s2, t_):
                link(nc.vector.tensor_tensor(s2, s_, s_, ALU.mult))
                link(nc.vector.tensor_scalar(t_, s2, 1.0 / 15, None, ALU.mult))
                for c in (13, 11, 9, 7, 5, 3):
                    link(nc.vector.scalar_tensor_tensor(out=t_, in0=t_, scalar=1.0 / c, in1=s2,
                                                        op0=ALU.add, op1=ALU.mult))
                link(nc.vector.scalar_tensor_tensor(out=t_, in0=t_, scalar=1.0, in1=s_,
                                                    op0=ALU.add, op1=ALU.mult))

            def flat(a):
                return a.rearrange("p a b -> p (a b)")

            def rope_angles():
                ve.wait_ge(pos_ready, 16)
                ve.wait_ge(tables_in, 16)
                ang, n_ = sq[:], acc_kv[:]
                link(nc.vector.tensor_copy(n_, pos_int[:]))
                link(nc.vector.tensor_scalar(ang, n_, tab[:, TABLE["inv_freq"]], None, ALU.mult))
                magic = 1.5 * 2.0 ** 23
                link(nc.vector.tensor_scalar(n_, ang, 1.0 / (2 * np.pi), magic, ALU.mult, ALU.add))
                link(nc.vector.tensor_scalar(n_, n_, magic, None, ALU.subtract))
                for part in TWO_PI:
                    link(nc.vector.scalar_tensor_tensor(out=ang, in0=n_, scalar=-part, in1=ang,
                                                        op0=ALU.mult, op1=ALU.add))
                pi = float(np.nextafter(np.float32(np.pi), np.float32(0)))
                link(nc.vector.tensor_scalar(ang, ang, pi, -pi, ALU.min, ALU.max))
                link(nc.vector.tensor_scalar(n_, ang, -1.0, None, ALU.mult))
                link(nc.vector.tensor_tensor(n_, ang, n_, ALU.max))
                nc.vector.tensor_scalar(n_, n_, -1.0, float(np.pi / 2), ALU.mult, ALU.add)\
                    .then_inc(rope_arg, 1)
                ve.wait_ge(rope_done, 2)

            def gla(c):
                ve.wait_ge(gla_logit, c + 1)
                for h in range(G_HEADS):
                    ins = nc.vector.tensor_scalar(g_x[:, h, :], pm[:, h // 2, (h % 2) * T:(h % 2 + 1) * T],
                                                  col(f"b_a{c}", h), None, ALU.add)
                ins.then_inc(gla_arg, 1)
                ve.wait_ge(gla_exp, c + 1)
                x_, e_, t_, s2 = flat(g_x), flat(g_e), flat(g_t), flat(g_s2)
                link(nc.vector.tensor_scalar(t_, e_, 2.0, None, ALU.add))
                link(nc.vector.reciprocal(t_, t_))
                link(nc.vector.tensor_tensor(e_, e_, t_, ALU.mult))
                link(nc.vector.tensor_scalar(x_, x_, 0.0, 1.0 / G_TAU, ALU.min, ALU.mult))
                log1p_over_2(e_, s2, t_)
                link(nc.vector.scalar_tensor_tensor(out=x_, in0=t_, scalar=-2.0 / G_TAU, in1=x_,
                                                    op0=ALU.mult, op1=ALU.add))
                for h in range(G_HEADS):
                    ins = nc.vector.tensor_tensor_scan(
                        out=b_cum[:, h, :], data0=power[:, 2:3].broadcast_to([P, T]),
                        data1=g_x[:, h, :], initial=0.0, op0=ALU.mult, op1=ALU.add)
                link(ins)
                masks = tab[:, TABLE["masks"]].rearrange("p (l t) -> p l t", t=P)
                for h in range(G_HEADS):
                    g = c * G_HEADS + h
                    b_ = b_cum[:, h, :]
                    for half in range(2):
                        for t in range(4):
                            span = 2 << (4 * half + t)
                            n_ = T // span
                            mid = b_.rearrange("p (n s) -> p n s", s=span)[:, :, span // 2 - 1:span // 2]
                            ins = nc.vector.tensor_tensor(
                                g_d[:, t, :].rearrange("p (n s) -> p n s", s=span),
                                b_.rearrange("p (n s) -> p n s", s=span),
                                mid.broadcast_to([P, n_, span]), ALU.subtract)
                        ins.then_inc(gla_diff, 1)
                        ve.wait_ge(gla_decay, 2 * g + half + 1)
                        if half:
                            ve.wait_ge(gla_scores, 2 * g + 1)
                        nc.vector.tensor_tensor(g_q, g_d, gqk[:, h:h + 1, :].broadcast_to([P, 4, T]),
                                                ALU.mult)
                        nc.vector.tensor_tensor(g_k, g_d,
                                                gqk[:, 4 + h:5 + h, :].broadcast_to([P, 4, T]),
                                                ALU.mult).then_inc(gla_qk, 1)
                        ve.wait_ge(gla_scores, 2 * g + half + 1)
                        for chunk in range(2):
                            ins = nc.vector.tensor_tensor(
                                g_m[chunk][:, 4 * half:4 * half + 4, :],
                                pm[:, chunk, :].rearrange("p (l t) -> p l t", t=P),
                                masks[:, 4 * half:4 * half + 4, :], ALU.mult)
                        if half == 0:
                            ins.then_inc(gla_scores_read, 1)
                        else:
                            ins.then_inc(gla_scores_read, 1)
                            ve.wait_ge(gla_scores_read, 2 * g + 2)
                    nc.vector.tensor_scalar(g_a[:, 2, :], pm[:, 2, 0:P], G_DK ** -0.5, None, ALU.mult)
                    for chunk in range(2):
                        ins = nc.vector.tensor_reduce(g_a[:, chunk, :],
                                                      g_m[chunk].rearrange("p l t -> p t l"),
                                                      mybir.AxisListType.X, ALU.add)
                    ins.then_inc(gla_mixed, 1)
                    norm(c + 2, f"gla{h}", g_rstd)
                    for j in range(2):
                        ins = nc.vector.scalar_tensor_tensor(
                            out=g_o[:, 2 * h + j, :], in0=pm[:, 2, j * T:(j + 1) * T],
                            scalar=col(f"o_g{c}", j), in1=g_rstd, op0=ALU.mult, op1=ALU.mult)
                    ins.then_inc(gla_normed, 1)

            def rotate(x1, x2, t1, t2, cos, sin):
                nc.vector.tensor_tensor(t1, x1, sin, ALU.mult)
                link(nc.vector.tensor_tensor(t2, x2, sin, ALU.mult))
                link(nc.vector.tensor_tensor(x1, x1, cos, ALU.mult))
                nc.vector.tensor_tensor(x1, x1, t2, ALU.subtract)
                link(nc.vector.tensor_tensor(x2, x2, cos, ALU.mult))
                return nc.vector.tensor_tensor(x2, x2, t1, ALU.add)

            def attention(c):
                x1, x2 = q_buf[:, 8:12:2, :], q_buf[:, 9:12:2, :]
                nc.vector.tensor_tensor(kr_sq, ka, ka, ALU.mult)
                nc.vector.tensor_tensor(r1, x1, x1, ALU.mult)
                link(nc.vector.tensor_tensor(r2, x2, x2, ALU.mult))
                ins = nc.vector.tensor_tensor(q_sq[:, 4:6, :], r1, r2, ALU.add)
                ins.then_inc(att_rsq, 1)
                ve.wait_ge(att_rsq, c + 1)
                ve.wait_ge(att_qms, 2 * c + 2)
                nc.vector.tensor_scalar(q_var, pm[:, 2, 0:16], 1.0 / QK, EPS, ALU.mult, ALU.add)\
                    .then_inc(att_qvar, 1)
                nc.vector.tensor_scalar(q_buf[:, 0:8, :], q_buf[:, 0:8, :], col(f"gq_nope{c}", 0),
                                        col(f"gk_nope{c}", 0), ALU.mult, ALU.mult)
                nc.vector.tensor_scalar(x1, x1, col(f"gq_r1{c}", 0), None, ALU.mult)
                link(nc.vector.tensor_scalar(x2, x2, col(f"gq_r2{c}", 0), None, ALU.mult))
                cos2, sin2 = (t[:, None, :].broadcast_to([P, 2, T]) for t in (rope_cos[:], rope_sin[:]))
                link(rotate(x1, x2, r1, r2, cos2, sin2))
                ve.wait_ge(att_rep, c + 1)
                nc.vector.tensor_scalar(kr[:, 0, :], pm[:, 0, 0:T], col(f"gk_r1{c}", 0), None, ALU.mult)
                link(nc.vector.tensor_scalar(kr[:, 1, :], pm[:, 0, T:2 * T], col(f"gk_r2{c}", 0), None,
                                             ALU.mult))
                rotate(kr[:, 0, :], kr[:, 1, :], r1[:, 0, :], r2[:, 0, :], rope_cos[:], rope_sin[:])\
                    .then_inc(att_roped, 1)
                ve.wait_ge(att_qrstd, c + 1)
                link(nc.vector.tensor_scalar(q_scale, q_rstd, QK ** -0.5, None, ALU.mult))
                neg = tab[:, TABLE["neg"]]
                for h in range(A_HEADS):
                    g, grp = c * A_HEADS + h, h // 4
                    sel = tab[:, TABLE["sel"].start + h % 4:TABLE["sel"].start + h % 4 + 1]
                    for part in range(2):
                        ins = nc.vector.tensor_scalar(qm[:, part, :], q_buf[:, 8 + 2 * grp + part, :], sel,
                                                      None, ALU.mult)
                    ins.then_inc(att_qm, 1)
                    norm(c + 2, f"k{h}", k_rstd)
                    ve.wait_ge(att_scores, g + 1)
                    nc.vector.tensor_tensor(att_s[:, 0:P], pm[:, 0, 0:P], k_rstd[:, 0:P], ALU.mult)
                    link(nc.vector.tensor_tensor(att_s[:, P:3 * P], pm[:, 0, P:3 * P], k_rstd, ALU.mult))
                    blocks = att_s.rearrange("p (b k) -> p b k", k=P)[:, 0:3:2, :]
                    link(nc.vector.tensor_tensor(blocks, blocks, neg[:, None, :].broadcast_to([P, 2, P]),
                                                 ALU.add))
                    nc.vector.tensor_reduce(s_max[:, 0:1], att_s[:, 0:P], mybir.AxisListType.X, ALU.max)
                    link(nc.vector.tensor_reduce(s_max[:, 1:2], att_s[:, P:3 * P],
                                                 mybir.AxisListType.X, ALU.max))
                    for tb in range(2):
                        ins = nc.vector.scalar_tensor_tensor(
                            out=s_bias[:, tb:tb + 1], in0=s_max[:, tb:tb + 1], scalar=-1.0,
                            in1=q_scale[:, tb * 8 + h:tb * 8 + h + 1], op0=ALU.mult, op1=ALU.mult)
                    ins.then_inc(att_max, 1)
                    ve.wait_ge(att_exp, 2 * g + 2)
                    link(nc.vector.reciprocal(s_inv, s_sum))
                    nc.vector.tensor_scalar(probs[:, 0:P], probs[:, 0:P], s_inv[:, 0:1], None, ALU.mult)
                    nc.vector.tensor_scalar(probs[:, P:3 * P], probs[:, P:3 * P], s_inv[:, 1:2], None,
                                            ALU.mult).then_inc(att_probs, 1)

            def spatial_gate(c):
                ve.wait_ge(sgu_ms, c + 1)
                nc.vector.tensor_scalar(s_col, pm[:, 2, 0:2], D / 1024, EPS, ALU.mult, ALU.add)\
                    .then_inc(sgu_var, 1)
                ve.wait_ge(sgu_in, 32 * (c + 1))
                nc.vector.tensor_tensor(w_st, w_st, tab[:, None, TABLE["tri"]].broadcast_to(
                    [P, S_GROUPS, P]), ALU.mult).then_inc(sgu_w, 1)
                for g in range(S_GROUPS):
                    ve.wait_ge(sgu_mix, c * S_GROUPS + g + 1)
                    nc.vector.scalar_tensor_tensor(
                        out=s_mix[:, g, :].rearrange("p (c t) -> p c t", t=P),
                        in0=pm[:, g % 2, 0:T].rearrange("p (c t) -> p c t", t=P),
                        scalar=col(f"v_g{c}", g), in1=b_st[:, g:g + 1, :].broadcast_to([P, 2, P]),
                        op0=ALU.mult, op1=ALU.add).then_inc(sgu_read, 1)
                ve.wait_ge(sgu_read, (c + 1) * S_GROUPS)

            nc.vector.memset(mean_d[:], 1.0 / D)
            nc.vector.memset(power[:, 0:1], -0.5)
            nc.vector.memset(power[:, 1:2], 0.5)
            nc.vector.memset(power[:, 2:3], 1.0)
            nc.vector.memset(power[:, 3:4], EPS)
            nc.vector.memset(taps_in[:], 0.0)
            nc.vector.memset(acc[:], 0.0)
            link(nc.vector.memset(win[:], 0.0))
            nc.vector.tensor_copy(rms[:, 0:1], win[:, 0, 0:1]).then_inc(consts_ready, 1)
            ve.wait_ge(consts_in, 32)
            nc.vector.tensor_scalar(half_b[:, 0, :], col("lru_ba", 0, NI), 0.5, None, ALU.mult)
            nc.vector.tensor_scalar(half_b[:, 1, :], col("lru_bx", 0, NI), 0.5, None, ALU.mult)\
                .then_inc(consts_ready, 1)
            for n in range(LOOKAHEAD):
                split_lo(n, n % SLOTS)
            ve.wait_ge(decay_e, 2)
            e, s2, s_, t_ = (tiny[:, j, :] for j in range(4))
            link(nc.vector.tensor_scalar(t_, e, 2.0, None, ALU.add))
            link(nc.vector.reciprocal(t_, t_))
            link(nc.vector.tensor_tensor(s_, e, t_, ALU.mult))
            log1p_over_2(s_, s2, t_)
            link(nc.vector.tensor_scalar(s_, col("lru_L", 0, NI), -LRU_C, 0.0, ALU.mult, ALU.max))
            link(nc.vector.scalar_tensor_tensor(out=decay[:], in0=t_, scalar=2 * LRU_C, in1=s_,
                                                op0=ALU.mult, op1=ALU.add))

            feeds = gelus = 0
            for n, s in enumerate(stages):
                l = s.layer
                if s.name == "za":
                    ve.wait_ge(att_done, (l - 1) * A_HEADS)
                if n:
                    wait(ve, pool_done, s.base["p"])
                if s.name in ("window", "conv"):
                    feed(feeds, f"g_pre{l}", (gated, "g_ple_out0", 0, "gate") if l else None)
                    feeds += 1
                if s.name == "conv":
                    ve.wait_ge(x_saved, 16)
                if s.name == "latent":
                    feed(feeds, f"norm_g{l - 2}", (gated, "g_ple_out1", 1, "gate") if l == 2 else None)
                    feeds += 1
                    if l == 2:
                        rope_angles()
                if s.name == "squared":
                    ve.wait_ge(x_loaded, 16 * (2 + l))
                    ve.wait_ge(p_hi, l + 1)
                    for k in range(NP_):
                        nc.vector.tensor_tensor(xs[:, k, T:2 * T], p_raw[:, k, :],
                                                xs[:, k, 0:T].bitcast(F32), ALU.subtract)\
                            .then_inc(p_ready, 1)
                if s.name == "gate":
                    feed(feeds, f"g_ple_in{l}", (o_buf, f"g_post{l}", l, "out"))
                    feeds += 1

                def first(i, j):
                    if s.name in ("window", "conv", "latent", "gate") and isinstance(i, int) and i == j == 0:
                        which = "ple" if s.name == "gate" else "enter"
                        norm(l, which, rstd_x)
                    m = i * s.width + j
                    v = val[:, j % 4, :]
                    if s.name == "window":
                        read_bank(s, i, j, v)
                        wait(ve, pool_done, m + (s.base["p"] - 3))
                        nc.vector.tensor_tensor(win[:, j % 4, PAD:], v, rstd_x[:], ALU.mult)\
                            .then_inc(val_ready, 1)
                    elif s.name == "pooled":
                        read_bank(s, i, j, v)
                        nc.vector.tensor_scalar(wide[:, m, :], v, col("pool_b", m),
                                                col("pool_scale", m), ALU.add, ALU.mult)
                    elif s.name in ("silu", "gate", "za", "zc", "zb", "vb", "ub", "latent"):
                        if s.name in ("latent", "vb", "ub"):
                            wait(ve, pool_done if s.name == "latent" else inner_ready,
                                 (s.base["p"] if s.name == "latent" else gelus * 8) + m - 3)
                        read_bank(s, i, j, v)
                        nc.vector.tensor_tensor(v, v, rstd_x[:], ALU.mult).then_inc(val_ready, 1)
                    elif s.name in ("rope_k", "gqk", "gv", "uq", "ukv"):
                        read_bank(s, i, j, v)
                        dest = {"rope_k": ka, "gqk": gqk, "gv": v_raw, "uq": q_buf, "ukv": k_buf}[s.name]
                        if s.name == "ukv" and m >= 8:
                            dest, m = v_raw, m - 8
                        dest = dest if s.name == "rope_k" else dest[:, m, :]
                        r_ = {"uq": rstd_r, "ukv": rstd_kv}.get(s.name, rstd_x)
                        nc.vector.tensor_tensor(dest, v, r_[:], ALU.mult).then_inc(val_ready, 1)
                    elif s.name == "mix":
                        pair, q = i * (s.width // 2) + j // 2, j // 2
                        v, a = val[:, 2 * (q % 2) + j % 2, :], act[:, q % 2, :]
                        if j % 2 == 0:
                            read_bank(s, i, j, v)
                            nc.vector.tensor_tensor(v, v, rstd_x[:], ALU.mult).then_inc(val_ready, 1)
                            return
                        m, branch = i * 4 + q // 3, q % 3
                        sum_ = act[:, 2 + (q // 3) % 2, :]
                        ve.wait_ge(act_ready, pair + (s.base["t"] + 1))
                        nc.vector.tensor_scalar(a, a, 0.5, 0.5, ALU.mult, ALU.add)
                        read_bank(s, i, j, v)
                        if branch == 0:
                            wait(ve, pool_done, m + (s.base["p"] - 1))
                            link(nc.vector.tensor_tensor(sum_, v, a, ALU.mult))
                        else:
                            link(nc.vector.tensor_tensor(v, v, a, ALU.mult))
                            ins = nc.vector.tensor_tensor(sum_, sum_, v, ALU.add)
                            if branch == 1:
                                link(ins)
                            else:
                                ins.then_inc(res_ready, 1)
                    elif s.name == "wo":
                        read_bank(s, i, j, v)
                        nc.vector.tensor_tensor(x_buf[:, m, :], x_buf[:, m, :], v, ALU.add)\
                            .then_inc(res_ready, 1)
                    elif s.name == "squared":
                        read_bank(s, i, j, o_buf[:, m, :])
                    elif s.name == "plain":
                        read_bank(s, i, j, gated[:, m, :])
                    elif s.name == "conv":
                        read_bank(s, i, j, v)
                        x_ = taps_in[:, j % 2, :]
                        link(nc.vector.tensor_tensor(x_[:, PAD:], v, rstd_x[:], ALU.mult))
                        o_ = wide[:, m, :]
                        link(nc.vector.tensor_scalar(o_, x_[:, PAD:], col(f"conv_w{TAPS - 1}", m),
                                                     col("conv_b", m), ALU.mult, ALU.add))
                        for tap in range(TAPS - 1):
                            at = PAD - (TAPS - 1) + tap
                            ins = nc.vector.scalar_tensor_tensor(
                                out=o_, in0=x_[:, at:at + T], scalar=col(f"conv_w{tap}", m), in1=o_,
                                op0=ALU.mult, op1=ALU.add)
                            if tap < TAPS - 2:
                                link(ins)
                        ins.then_inc(res_ready, 1)

                def second(i, j):
                    m = i * s.width + j
                    v, a = val[:, j % 4, :], act[:, j % 4, :]
                    if s.name == "window":
                        ve.wait_ge(pool_done, m + (s.base["p"] + 1))
                        link(nc.vector.tensor_copy(inner[:, m, 0:T], a))
                        nc.vector.tensor_tensor(inner[:, m, T:2 * T], a,
                                                inner[:, m, 0:T].bitcast(F32), ALU.subtract)\
                            .then_inc(tile_split, 1)
                    elif s.name == "latent":
                        ve.wait_ge(act_ready, m + (s.base["t"] + 1))
                        nc.vector.scalar_tensor_tensor(
                            out=latent[:, m, T:2 * T], in0=v,
                            scalar=col(("cq_g%d" if m < 4 else "ckv_g%d") % (l - 2), m % 4),
                            in1=latent[:, m, 0:T].bitcast(F32), op0=ALU.mult, op1=ALU.subtract)\
                            .then_inc(res_ready, 1)
                    elif s.name in ("silu", "za", "zc", "zb"):
                        y = {"silu": wide, "za": q_buf, "zc": g_o, "zb": s_mix}[s.name]
                        ve.wait_ge(act_ready, m + (s.base["t"] + 1))
                        link(nc.vector.scalar_tensor_tensor(out=a, in0=a, scalar=1.0, in1=v,
                                                            op0=ALU.add, op1=ALU.mult))
                        nc.vector.scalar_tensor_tensor(out=a, in0=a, scalar=0.5, in1=y[:, m, :],
                                                       op0=ALU.mult, op1=ALU.mult).then_inc(res_ready, 1)
                    elif s.name == "gate":
                        ve.wait_ge(act_ready, m + (s.base["t"] + 1))
                        link(nc.vector.tensor_scalar(a, a, 0.5, 0.5, ALU.mult, ALU.add))
                        nc.vector.tensor_tensor(gated[:, m, :], gated[:, m, :], a, ALU.mult)\
                            .then_inc(res_ready, 1)

                def gelu(m):
                    v, a = val[:, m % 4, :], act[:, m % 4, :]
                    ve.wait_ge(act_ready, m + (s.base["t"] + 1))
                    link(nc.vector.scalar_tensor_tensor(out=a, in0=a, scalar=1.0, in1=v,
                                                        op0=ALU.add, op1=ALU.mult))
                    if s.name == "vb":
                        ins = nc.vector.tensor_scalar(s_v[:, m, :], a, 0.5, None, ALU.mult)
                    else:
                        ins = nc.vector.scalar_tensor_tensor(
                            out=s_mix[:, m, :], in0=a, scalar=0.5, in1=s_mix[:, m, :], op0=ALU.mult,
                            op1=ALU.mult)
                    ins.then_inc(res_ready, 1)

                def gates(i, h):
                    t, m = i * 4 + h, i * 8 + 2 * h
                    ve.wait_ge(lru_sig, t * 4 + 4)
                    link(nc.vector.tensor_scalar(lru_act[:, :, :], lru_act[:, :, :], 0.5, 0.5,
                                                 ALU.mult, ALU.add))
                    for j in range(2):
                        d = decay[:, bass.ds(m + j, 1)] if not isinstance(m, int) else \
                            decay[:, m + j:m + j + 1]
                        ins = nc.vector.tensor_scalar(val[:, j, :], lru_act[:, j, :], d, None, ALU.mult)
                    ins.then_inc(lru_p, 1)

                def one_minus_a2(i, h):
                    t = i * 4 + h
                    ve.wait_ge(lru_at, t * 2 + 2)
                    link(nc.vector.tensor_tensor(val[:, 0:2, :], lru_a[:, :, :], lru_a[:, :, :], ALU.mult))
                    nc.vector.scalar_tensor_tensor(out=lru_act[:, 0:2, :], in0=val[:, 0:2, :], scalar=1.0,
                                                   in1=lru_act[:, 0:2, :], op0=ALU.add, op1=ALU.mult)\
                        .then_inc(lru_m, 1)

                def scan(i, h):
                    t, m = i * 4 + h, i * 8 + 2 * h
                    ve.wait_ge(lru_b, t + 1)
                    for j in range(2):
                        ins = nc.vector.tensor_tensor_scan(
                            out=wide[:, m + j, :], data0=lru_a[:, j, :], data1=lru_act[:, j, :],
                            initial=0.0, op0=ALU.mult, op1=ALU.add)
                    ins.then_inc(lru_y, 1)
                    ve.wait_ge(lru_y, t + 1)

                def read_z(i, h, j):
                    v = val[:, 2 + j, :]
                    read_bank(s, i, 6 * h + 4 + j, v)
                    nc.vector.tensor_tensor(v, v, rstd_x[:], ALU.mult).then_inc(val_ready, 1)

                def finish_z(i, h, j):
                    z = i * 8 + 2 * h + j
                    ve.wait_ge(act_ready, z + (s.base["t"] + 1))
                    a, v = act[:, j, :], val[:, 2 + j, :]
                    link(nc.vector.scalar_tensor_tensor(out=a, in0=a, scalar=1.0, in1=v,
                                                        op0=ALU.add, op1=ALU.mult))
                    nc.vector.scalar_tensor_tensor(out=a, in0=a, scalar=0.5, in1=wide[:, z, :],
                                                   op0=ALU.mult, op1=ALU.mult).then_inc(res_ready, 1)

                def lru_unit(i, u):
                    h, q = divmod(u, 5)
                    if q == 0:
                        if not (isinstance(i, int) and i == 0 and h == 0):
                            finish_z(*((i, h - 1) if h else (i - 1, 3)), 1)
                        for j in range(4):
                            read_bank(s, i, 6 * h + j, val[:, j, :])
                        gates(i, h)
                    elif q == 1:
                        one_minus_a2(i, h)
                    elif q == 2:
                        read_z(i, h, 0)
                    elif q == 3:
                        scan(i, h)
                    else:
                        finish_z(i, h, 0)
                        read_z(i, h, 1)

                def turn(i):
                    for u in range(s.units):
                        n_ = s.unit0 + u + LOOKAHEAD
                        split_lo(i * s.units + n_, n_ % SLOTS)
                        if s.name == "lru":
                            lru_unit(i, u)
                            continue
                        for j, p in enumerate(s.products):
                            if p.last_unit == u:
                                first(i, j)
                                if s.name in ("vb", "ub"):
                                    if i * s.width + j >= 2:
                                        gelu(i * s.width + j - 2)
                                elif not (isinstance(i, int) and i == 0 and j == 0):
                                    second(*before(s, i, j))

                per = {"window": 4, "silu": 4, "gate": 4, "conv": 16, "lru": 16, "za": 4, "zc": 4,
                       "zb": 4, "mix": 4 * 4}.get(s.name, 0)
                run_stage(ve, s, turn, per, dve_chain)
                if s.name == "lru":
                    finish_z(s.turns - 1, 3, 1)
                elif s.name in ("window", "silu", "gate", "latent", "za", "zc", "zb"):
                    second(s.turns - 1, s.width - 1)
                elif s.name in ("vb", "ub"):
                    gelu(6)
                    gelu(7)
                    gelus += 1
                if s.name == "rope_k":
                    norm(l, "cq", rstd_r)
                    norm(l, "ckv", rstd_kv)
                if s.name == "gv":
                    gla(l - 2)
                if s.name == "ukv":
                    attention(l - 2)
                if s.name == "vb":
                    spatial_gate(l - 2)

        @block.gpsimd
        def _(gp):
            link = lambda ins: pool_chain.link(gp, ins)

            def feed(f):
                for b in range(4):
                    gp.wait_ge(x_sq, f * 4 + b + 1)
                    if b == 0:
                        ins = nc.gpsimd.tensor_copy(act[:, :, :], val[:, :, :])
                    else:
                        ins = nc.gpsimd.tensor_tensor(act[:, :, :], act[:, :, :], val[:, :, :], ALU.add)
                    ins.then_inc(sq_added, 1)
                    gp.wait_ge(sq_added, f * 4 + b + 1)

            def split(dest, source):
                link(nc.gpsimd.tensor_copy(dest[:, 0:T], source))
                nc.gpsimd.tensor_tensor(dest[:, T:2 * T], source, dest[:, 0:T].bitcast(F32),
                                        ALU.subtract).then_inc(pool_done, 1)

            gp.wait_ge(consts_ready, 1)
            gp.wait_ge(consts_in, 32)
            feeds = 0
            for n, s in enumerate(stages):
                l = s.layer
                if s.name in ("window", "conv"):
                    feed(feeds)
                    feeds += 1
                if s.name == "gate":
                    feed(feeds)
                    feeds += 1
                if s.name == "latent":
                    feed(feeds)
                    feeds += 1
                    if l == 2:
                        gp.wait_ge(rope_done, 2)
                    link(nc.gpsimd.memset(acc_kv[:], 0.0))
                if s.name in ("squared", "gate", "latent", "vb"):
                    before_ = {"squared": "out", "gate": "gate", "latent": "cq"}
                    if s.name == "vb":
                        gp.wait_ge(ms_ready, norms[l, f"k{A_HEADS - 1}"] + 1)
                    else:
                        wait(gp, ms_ready, norms[l, before_[s.name]])
                    wait(gp, sgu_ms, l - 2)
                    link(nc.gpsimd.memset(acc[:], 0.0))

                def post(i, j, group=None):
                    m = i * (4 if s.name == "mix" else s.width) + j
                    wait(gp, pool_done, m + s.base["p"])
                    if s.name == "window":
                        x_ = win[:, j % 4, :]
                        gp.wait_ge(val_ready, m + (s.base["v"] + 1))
                        wait(gp, tile_split, m - 3)
                        src = x_
                        for level in range(group + 1):
                            dst = win[:, 4 + level % 2, :]
                            back = PAD - (1 << level)
                            link(nc.gpsimd.tensor_tensor(dst[:, PAD:], src[:, PAD:],
                                                         src[:, back:back + T], ALU.add))
                            src = dst
                        link(nc.gpsimd.tensor_tensor(src[:, PAD:], src[:, PAD:],
                                                     inv_count[:, group, :], ALU.mult))
                        nc.gpsimd.tensor_tensor(act[:, j % 4, :], src[:, PAD:], x_[:, PAD:],
                                                ALU.subtract).then_inc(pool_done, 1)
                    elif s.name in ("silu", "za", "zc", "zb"):
                        gp.wait_ge(res_ready, m + (s.base["q"] + 1))
                        first_tile = {"za": 0, "zb": 8, "zc": 16}.get(s.name)
                        split(inner[:, m, :] if s.name == "silu" else y_abc[:, m + first_tile, :],
                              act[:, j % 4, :])
                    elif s.name == "mix":
                        gp.wait_ge(res_ready, m + (s.base["q"] + 1))
                        split(merged[:, m, :], act[:, 2 + j % 2, :])
                    elif s.name == "latent":
                        gp.wait_ge(val_ready, m + (s.base["v"] + 1))
                        a, sum_ = val[:, j % 4, :], (acc if m < 4 else acc_kv)[:]
                        link(nc.gpsimd.tensor_tensor(sq[:], a, a, ALU.mult))
                        nc.gpsimd.tensor_tensor(sum_, sum_, sq[:], ALU.add).then_inc(pool_done, 1)
                        gp.wait_ge(pool_done, m + (s.base["p"] + 1))
                    elif s.name == "conv":
                        gp.wait_ge(res_ready, m + (s.base["q"] + 1))
                        split(inner[:, m, :], wide[:, m, :])
                    elif s.name in ("squared", "gate"):
                        if s.name == "squared":
                            gp.wait_ge(bank_free, bank_of(s, i, j) + 1)
                            a = o_buf[:, m, :]
                        else:
                            gp.wait_ge(res_ready, m + (s.base["q"] + 1))
                            a = gated[:, m, :]
                        link(nc.gpsimd.tensor_tensor(sq[:], a, a, ALU.mult))
                        nc.gpsimd.tensor_tensor(acc[:], acc[:], sq[:], ALU.add).then_inc(pool_done, 1)
                        gp.wait_ge(pool_done, m + (s.base["p"] + 1))

                def turn(i):
                    if s.name == "lru":
                        for h in range(4):
                            t, m = i * 4 + h, i * 8 + 2 * h
                            gp.wait_ge(lru_root, t + 1)
                            b_ = lru_act[:, 0:2, :]
                            link(nc.gpsimd.tensor_tensor(b_, b_, lru_act[:, 2:4, :], ALU.mult))
                            nc.gpsimd.tensor_tensor(b_, b_, wide[:, bass.ds(m, 2), :]
                                                    if not isinstance(m, int) else wide[:, m:m + 2, :],
                                                    ALU.mult).then_inc(lru_b, 1)
                            for j in range(2):
                                z = m + j
                                wait(gp, pool_done, z + s.base["p"])
                                gp.wait_ge(res_ready, z + (s.base["q"] + 1))
                                split(inner[:, z, :], act[:, j, :])
                    elif s.name in ("vb", "ub"):
                        for j in range(s.width):
                            gelu_inner(i * s.width + j)
                            if s.name == "vb" and i * s.width + j >= 2:
                                square_v(i * s.width + j - 2)
                    else:
                        for j in range(4 if s.name == "mix" else s.width):
                            post(i, j)

                def gelu_inner(m):
                    v, a = val[:, m % 4, :], act[:, m % 4, :]
                    gp.wait_ge(val_ready, m + (s.base["v"] + 1))
                    wait(gp, res_ready, m + (s.base["q"] - 3))
                    link(nc.gpsimd.tensor_tensor(a, v, v, ALU.mult))
                    link(nc.gpsimd.tensor_scalar(a, a, GELU_C, 1.0, ALU.mult, ALU.add))
                    nc.gpsimd.tensor_tensor(a, a, v, ALU.mult).then_inc(inner_ready, 1)

                def square_v(m):
                    gp.wait_ge(res_ready, m + (s.base["q"] + 1))
                    wait(gp, pool_done, m + s.base["p"])
                    link(nc.gpsimd.tensor_tensor(sq[:], s_v[:, m, :], s_v[:, m, :], ALU.mult))
                    nc.gpsimd.tensor_tensor(acc[:], acc[:], sq[:], ALU.add).then_inc(pool_done, 1)

                if s.name == "window":
                    for group in range(4):
                        def group_turn(i):
                            for j in range(4):
                                post(i, j, group)
                        if group == 0:
                            group_turn(0)
                            group_turn(1)
                        else:
                            with gp.Fori(2 * group, 2 * group + 2) as i:
                                with pool_chain.loop(i - 2 * group, 2, 4 * (group + 2)):
                                    group_turn(i)
                elif s.name not in ("pooled", "plain", "rope_k", "gqk", "gv", "uq", "ukv", "wo"):
                    run_stage(gp, s, turn, 12 if s.name == "lru" else 4, pool_chain)
                if s.name == "vb":
                    square_v(6)
                    square_v(7)
                    gp.wait_ge(sgu_var, l - 1)
                    nc.gpsimd.tensor_tensor(s_rstd, s_col, power[:, 0:1].broadcast_to([P, 2]), ALU.pow)\
                        .then_inc(sgu_rstd, 1)
                if s.name == "ukv":
                    gp.wait_ge(att_qvar, l - 1)
                    nc.gpsimd.tensor_tensor(q_rstd, q_var, power[:, 0:1].broadcast_to([P, 16]), ALU.pow)\
                        .then_inc(att_qrstd, 1)


def feature_major(a):
    t, f = a.shape
    return a.reshape(t, f // P, P).transpose(2, 1, 0)


def tiles(w):
    k, n = w.shape
    return w.reshape(k // P, P, n // P, P).transpose(2, 0, 1, 3)


def stream(parts):
    flat = np.concatenate([p.reshape(-1, P, P) for p in parts])
    return np.ascontiguousarray(flat.reshape(-1, UNIT_TILES, P, P).transpose(0, 2, 1, 3)
                                .reshape(-1, P, UNIT))


def constant_tables():
    i = np.arange(P)
    t = {"ident": np.eye(P)}
    masks = []
    for level in list(range(1, LEVELS)) + [0]:
        if level == 0:
            m = i[:, None] == i[None]
        else:
            half = i >> (level - 1)
            m = ((half[:, None] + 1) == half[None]) & (half[:, None] % 2 == 0)
        masks.append(m * G_DK ** -0.5)
    t["masks"] = np.concatenate(masks, 1)
    t["tri"] = i[:, None] <= i[None]
    t["neg"] = np.where(i[:, None] >= i[None], 0.0, NEG)
    t["sel"] = (i[:, None] // 32) == np.arange(4)[None]
    t["rep1"] = (i[:, None] < 32) & (i[:, None] == i[None] % 32)
    t["rep2"] = (i[:, None] >= 32) & (i[:, None] < 64) & (i[:, None] - 32 == i[None] % 32)
    t["rope_rows"] = np.repeat((i[:, None] < ROPE) / D, P, 1)
    exps = np.arange(0, ROPE, 2, dtype=np.float32) / np.float32(ROPE)
    t["inv_freq"] = np.tile(np.float32(1.0) / np.float32(10000.0) ** exps, 4)[:, None]
    return np.ascontiguousarray(
        np.concatenate([np.broadcast_to(t[k], (P, n)) for k, n in TABLES], 1).astype(np.float32))


def kernel(**inputs):
    import concourse.bacc as bacc
    from concourse.bass_utils import run_bass_kernel_spmd

    a = {k: np.asarray(v) for k, v in inputs.items()}
    parts = []
    for l in range(2):
        w_u, w_z = tiles(a["w_in"][l][:, :DI]), tiles(a["w_in"][l][:, DI:])
        parts.append(w_u)
        if l == 0:
            parts += [tiles(a["pool_w"][0, g]) for g in range(4)]
            parts.append(w_z)
        else:
            for h in range(HEADS):
                parts += [tiles(a["lru_wa"][0, h]), tiles(a["lru_wx"][0, h]), w_z[2 * h:2 * h + 2]]
        parts += [tiles(a["w_out"][l]), tiles(a["w_ple"][l]), tiles(a["w_ple_gate"][l])]
    sizes = (RANK, RANK, ROPE, 1024, 1024, 1024, 1024, 512, 512, 1024, 16, 1024, 3 * D)
    starts = np.cumsum((0,) + sizes)
    names = ("cq", "ckv", "kr", "za", "ub", "vb", "zb", "gq", "gk", "gv", "ar", "zc", "gate")
    part = {n: slice(starts[i], starts[i + 1]) for i, n in enumerate(names)}
    for l in range(2):
        w = a["w_in_2"][l]
        kr_ar = np.concatenate([w[:, part["kr"]], w[:, part["ar"]], np.zeros((D, 48), np.float32)], 1)
        parts += [tiles(w[:, part["cq"]]), tiles(w[:, part["ckv"]]), tiles(kr_ar),
                  tiles(w[:, part["gq"]]), tiles(w[:, part["gk"]]), tiles(w[:, part["gv"]])]
        w_q = a["mla_w_uq_2"][l].reshape(RANK, A_HEADS, QK)
        half = ROPE // 2
        parts.append(tiles(np.concatenate(
            [w_q[:, :, :NOPE].reshape(RANK, -1)]
            + [w_q[:, g:g + 4, at:at + half].reshape(RANK, -1)
               for g in (0, 4) for at in (NOPE, NOPE + half)], 1)))
        w_kv = a["mla_w_ukv_2"][l].reshape(RANK, A_HEADS, 2 * P)
        parts.append(tiles(np.concatenate([w_kv[:, :, :P].reshape(RANK, -1),
                                           w_kv[:, :, P:].reshape(RANK, -1)], 1)))
        parts += [tiles(w[:, part[n]]) for n in ("za", "zc", "vb", "ub", "zb")]
        gates = tiles(w[:, part["gate"]]).reshape(3, ND, ND, P, P)
        branches = [tiles(a["w_branch_2"][l, b]) for b in range(3)]
        for m in range(ND):
            for b in range(3):
                parts += [gates[b, m], branches[b][m]]
        parts.append(tiles(a["w_out_2"][l]))
    weights = stream(parts)

    def columns(v):
        return v.reshape(-1, P).T

    named = {}
    for l in range(2):
        for k in ("g_pre", "g_post", "g_ple_in", "g_ple_out"):
            named[f"{k}{l}"] = a[k][l]
    for k in ("pool_b", "pool_scale", "conv_b", "lru_ba", "lru_bx", "lru_L"):
        named[k] = a[k][0]
    for k in range(TAPS):
        named[f"conv_w{k}"] = a["conv_w"][0, k]
    for l in range(2):
        named[f"norm_g{l}"] = a["norm_g_2"][l]
        named[f"cq_g{l}"], named[f"ckv_g{l}"] = a["mla_cq_norm_2"][l], a["mla_ckv_norm_2"][l]
        named[f"v_g{l}"], named[f"o_g{l}"] = a["sgu_v_norm_2"][l], a["gla_o_norm_2"][l]
        named[f"b_a{l}"] = a["gla_b_a_2"][l]
        for k, g in (("q", a["mla_q_norm_2"][l]), ("k", a["mla_k_norm_2"][l])):
            named[f"g{k}_nope{l}"] = g[:NOPE]
            named[f"g{k}_r1{l}"] = np.tile(g[NOPE:NOPE + ROPE // 2], 4)
            named[f"g{k}_r2{l}"] = np.tile(g[NOPE + ROPE // 2:], 4)
    w_a2 = np.zeros((2, P, 512), np.float32)
    w_a2[:, ROPE:ROPE + 16] = a["gla_w_a2_2"]
    channels = np.ascontiguousarray(np.concatenate([columns(named[k]) for k, _ in CHANNELS], 1))
    counts = np.stack([1.0 / np.minimum(np.arange(1, T + 1), w) for w in POOL_WINDOWS])
    arrays = {
        "weights": weights,
        "x_in": np.ascontiguousarray(feature_major(a["x"][0])),
        "p_in": np.ascontiguousarray(np.stack([feature_major(a["p"][l, 0]) for l in range(2)])),
        "channels": channels,
        "tables": constant_tables(),
        "positions": np.ascontiguousarray(np.broadcast_to(a["positions_2"][0], (P, T))),
        "w_a2": w_a2,
        "w_s": np.ascontiguousarray(a["sgu_w_s_2"].transpose(0, 3, 1, 2)),
        "b_s": np.ascontiguousarray(np.broadcast_to(a["sgu_b_s_2"][:, None], (2, P, S_GROUPS, P))),
        "inv_counts": np.ascontiguousarray(
            np.broadcast_to(counts.astype(np.float32)[None], (P, 4, T))),
    }
    nc = bacc.Bacc("TRN2", target_bir_lowering=False, num_devices=1)
    order = ("weights", "x_in", "p_in", "channels", "inv_counts", "tables", "positions", "w_a2", "w_s",
             "b_s")
    aps = [nc.dram_tensor(k, arrays[k].shape, mybir.dt.from_np(arrays[k].dtype),
                          kind="ExternalInput").ap() for k in order]
    scratch = nc.dram_tensor("x_scratch", (P, ND, T), F32, kind="Internal").ap()
    out = nc.dram_tensor("out_x", (P, ND, T), F32, kind="ExternalOutput").ap()
    build(nc, *aps, scratch, out)
    r = run_bass_kernel_spmd(nc, [arrays], core_ids=[0])
    got = r.results[0]["out_x"]
    return np.ascontiguousarray(got.transpose(2, 1, 0)).reshape(1, T, D)
```

```python
from contextlib import ExitStack, contextmanager

import numpy as np

import concourse.bass as bass
from concourse import mybir

P = 128
T = 256
D = 2048
DI = 4096
ND = D // P
NI = DI // P
PLE = 256
NP_ = PLE // P
UNIT_TILES = 8
UNIT = UNIT_TILES * P
SLOTS = 4
LOOKAHEAD = SLOTS - 1
BANKS = 4
EPS = 1e-6
POOL_WINDOWS = (2, 4, 8, 16)
PAD = 16
TAPS = 4
HEADS = 16
A_HEADS, NOPE, ROPE, RANK = 8, 128, 64, 512
QK = NOPE + ROPE
G_HEADS, G_DK, G_TAU, LEVELS = 4, 128, 16.0, 8
S_GROUPS = 8
NEG = -1.0e30
GELU_A, GELU_C = 0.7978845608028654, 0.044715
TWO_PI = (6.28125, 0.0019353071693331003, 1.0253131677018246e-11)
LRU_C = 8.0

F32 = mybir.dt.float32
F32R = mybir.dt.float32r
ALU = mybir.AluOpType
ACT = mybir.ActivationFunctionType


class Product:

    def __init__(self, depth, operand):
        self.depth, self.operand = depth, operand


class Stage:

    def __init__(self, name, products, turns):
        self.name, self.products, self.turns = name, products, turns
        tile = 0
        for p in products:
            p.first_tile = tile
            tile += p.depth
            p.last_unit = (tile - 1) // UNIT_TILES
        assert tile % UNIT_TILES == 0
        self.units = tile // UNIT_TILES
        self.width = len(products)


class Chain:

    def __init__(self, sem):
        self.sem, self.base, self.step, self.turn, self.per = sem, 0, 0, 0, 0

    def link(self, eng, ins):
        ins.then_inc(self.sem, 1)
        self.step += 1
        eng.wait_ge(self.sem, self.base + self.turn * self.per + self.step)

    @contextmanager
    def loop(self, turn, count, per):
        self.base += self.step
        self.step, self.turn, self.per = 0, turn, per
        yield
        assert self.step == per, (self.step, per)
        self.base += count * per
        self.step, self.turn, self.per = 0, 0, 0


def wait(eng, sem, value):
    if not isinstance(value, int) or value > 0:
        eng.wait_ge(sem, value)


CHANNELS = (
    [(f"g_pre{l}", ND) for l in range(2)] + [(f"g_post{l}", ND) for l in range(2)]
    + [(f"g_ple_in{l}", ND) for l in range(2)] + [(f"g_ple_out{l}", ND) for l in range(2)]
    + [("pool_b", NI), ("pool_scale", NI)] + [(f"conv_w{k}", NI) for k in range(TAPS)]
    + [("conv_b", NI), ("lru_ba", NI), ("lru_bx", NI), ("lru_L", NI)]
    + [(f"{k}{l}", n) for l in range(2) for k, n in (
        ("norm_g", ND), ("cq_g", 4), ("ckv_g", 4), ("v_g", 8), ("o_g", 2), ("b_a", 4),
        ("gq_nope", 1), ("gk_nope", 1), ("gq_r1", 1), ("gq_r2", 1), ("gk_r1", 1), ("gk_r2", 1))]
)
COLUMN, _at = {}, 0
for _name, _n in CHANNELS:
    COLUMN[_name] = _at
    _at += _n
N_CHANNELS = _at
TABLES = [("ident", P), ("masks", LEVELS * P), ("tri", P), ("neg", P), ("sel", 4), ("rep1", P),
          ("rep2", P), ("rope_rows", 4), ("inv_freq", 1)]
TABLE, _at = {}, 0
for _name, _n in TABLES:
    TABLE[_name] = slice(_at, _at + _n)
    _at += _n
N_TABLES = _at


def build(nc, weights, x_in, p_in, channels, inv_counts, tables, positions, w_a2, w_s, b_s, x_scratch,
          out):
    with ExitStack() as ctx:
        def sb(name, shape, dt=F32, into=ctx):
            return into.enter_context(nc.sbuf_tensor(name, shape, dt))

        def sem(name):
            return ctx.enter_context(nc.semaphore(name))

        raw = sb("raw", [P, SLOTS, UNIT])
        w_hi = sb("w_hi", [P, SLOTS, UNIT], F32R)
        w_lo = sb("w_lo", [P, SLOTS, UNIT], F32R)
        xs = sb("xs", [P, ND, 2 * T], F32R)
        small = sb("small", [P, 2, T])
        val = sb("val", [P, 4, T])
        act = sb("act", [P, 4, T])
        acc = sb("acc", [P, T])
        sq = sb("sq", [P, T])
        rstd_x = sb("rstd_x", [P, T])
        rstd_r = sb("rstd_r", [P, T])
        rms = sb("rms", [P, T])
        mean_d = sb("mean_d", [P, P])
        power = sb("power", [P, 4])
        ones_col, eps_col = power[:, 2:3], power[:, 3:4]
        chan = sb("chan", [P, N_CHANNELS])
        with ExitStack() as temps:
            taps_in = sb("taps_in", [P, 2, PAD + T], F32, temps)
            p_raw = sb("p_raw", [P, NP_, T], F32, temps)
            lru_act = sb("lru_act", [P, 4, T], F32, temps)
            lru_a = sb("lru_a", [P, 2, T], F32, temps)
            decay = sb("decay", [P, NI], F32, temps)
            half_b = sb("half_b", [P, 2, NI], F32, temps)
            tiny = sb("tiny", [P, 4, NI], F32, temps)
        tab = sb("tab", [P, N_TABLES])
        acc_kv = sb("acc_kv", [P, T])
        rstd_kv = sb("rstd_kv", [P, T])
        rope_cos, rope_sin = sb("rope_cos", [P, T]), sb("rope_sin", [P, T])
        with ExitStack() as block1:
            inner = sb("inner", [P, NI, 2 * T], F32R, block1)
            wide = sb("wide", [P, NI, T], F32, block1)
        with ExitStack() as overlay:
            gated = sb("gated", [P, ND, T], F32, overlay)
        with ExitStack() as overlay:
            sb("inner_again", [P, NI, 2 * T], F32R, overlay)
            win = sb("win", [P, 6, PAD + T], F32, overlay)
            inv_count = sb("inv_count", [P, 4, T], F32, overlay)
        o_buf, x_buf = wide[:, 0:ND, :], wide[:, ND:NI, :]
        with ExitStack() as overlay:
            y_abc = sb("y_abc", [P, 24, 2 * T], F32R, overlay)
            scr = sb("scr", [P, 8192], F32, overlay)
        with ExitStack() as overlay:
            latent = sb("latent", [P, 8, 2 * T], F32R, overlay)
            scr2 = sb("scr2", [P, 8192], F32, overlay)
            merged = sb("merged", [P, ND, 2 * T], F32R, overlay)
        with ExitStack() as overlay:
            pos_int = sb("pos_int", [P, T], mybir.dt.int32, overlay)

        def view(buf, at, *shape):
            n = int(np.prod(shape))
            part = buf[:, at:at + n]
            if len(shape) == 2:
                part = part.rearrange("p (a b) -> p a b", b=shape[1])
            return part

        gqk = view(scr2, 0, 8, T)
        b_cum = view(scr2, 2048, 4, T)
        g_x, g_e = view(scr2, 3072, 4, T), view(scr2, 4096, 4, T)
        g_d = [g_x, g_e]
        g_q = [view(scr2, 5120, 4, T), view(scr, 4096, 4, T)]
        g_m = [view(scr2, 6144, LEVELS, P), view(scr2, 7168, LEVELS, P)]
        g_v = view(scr, 0, 2, 1024)
        g_o = view(scr, 2048, 8, T)
        v_raw = view(scr, 4096, 8, T)
        wa2 = view(scr, 6144, 512)
        g_a = view(scr, 6656, 3, P)
        g_sq = view(scr, 7040, 2, T)
        g_rstd = view(scr, 7552, T)
        ka = view(scr, 7808, T)
        q_buf = view(scr2, 0, 12, T)
        k_buf = view(scr2, 3072, 8, T)
        kr = view(scr2, 5120, 2, T)
        r1, r2 = view(scr2, 5632, 2, T), view(scr2, 6144, 2, T)
        qm = [view(scr2, 6656, 2, T), view(scr2, 5632, 2, T)]
        rms_cols, rstd_cols = view(scr2, 7680, 32), view(scr2, 7712, 32)
        q_scale = view(scr2, 7744, 16)
        s_max, s_bias, s_sum, s_inv = (view(scr2, a, 2, 2) for a in (7760, 7764, 7768, 7772))
        kr_sq = view(scr2, 7936, T)
        a_v = view(scr, 0, 2, 1024)
        q_sq = view(scr, 6144, 6, T)
        diag = view(scr, 6144, 8, P)
        k_rstd = view(scr, 4096, 8, T)
        probs = [view(scr, 6144, 384), view(scr, 6528, 384)]
        att_s = [view(scr, 6912, 384), view(scr2, 7168, 384)]
        probs_t = view(scr, 7296, 384)
        s_v = view(scr, 0, 8, T)
        s_vt = view(scr, 2048, 2, 1024)
        s_mix = view(scr, 4096, 8, T)
        w_st = view(scr, 6144, S_GROUPS, P)
        s_col, s_rstd = view(scr, 7168, 2), view(scr, 7170, 2)
        b_st = view(scr2, 0, S_GROUPS, P)

        banks = ctx.enter_context(nc.psum_tensor("banks", [P, BANKS, 2 * T], F32))
        ms_bank = ctx.enter_context(nc.psum_tensor("ms_bank", [P, 2 * T], F32))
        pm = ctx.enter_context(nc.psum_tensor("pm", [P, 3, 2 * T], F32))

        raw_in = [sem(f"raw_in{s}") for s in range(SLOTS)]
        hi_done, lo_done, unit_used = sem("hi_done"), sem("lo_done"), sem("unit_used")
        small_ready, bank_free = sem("small_ready"), sem("bank_free")
        val_ready, act_ready, res_ready = sem("val_ready"), sem("act_ready"), sem("res_ready")
        pool_done, tile_split = sem("pool_done"), sem("tile_split")
        consts_in, consts_ready, x_loaded, x_saved = (sem("consts_in"), sem("consts_ready"),
                                                      sem("x_loaded"), sem("x_saved"))
        p_loaded, p_hi, p_ready = sem("p_loaded"), sem("p_hi"), sem("p_ready")
        x_updated, x_hi, x_sq, xs_ready = sem("x_updated"), sem("x_hi"), sem("x_sq"), sem("xs_ready")
        ms_ready, root_ready, rstd_ready = (sem("ms_ready"),
                                                      sem("root_ready"), sem("rstd_ready"))
        sq_added = sem("sq_added")
        lru_root, lru_sig, lru_p, lru_at, lru_m, lru_b, lru_y = (
            sem("lru_root"), sem("lru_sig"), sem("lru_p"), sem("lru_at"), sem("lru_m"), sem("lru_b"),
            sem("lru_y"))
        decay_e, out_done = sem("decay_e"), sem("out_done")
        tables_in, small_in, pos_ready, rope_arg, rope_done = (
            sem("tables_in"), sem("small_in"), sem("pos_ready"), sem("rope_arg"), sem("rope_done"))
        inner_ready = sem("inner_ready")
        turned, turn_read = sem("turned"), sem("turn_read")
        gla_logit, gla_arg, gla_exp = sem("gla_logit"), sem("gla_arg"), sem("gla_exp")
        gla_scores_read = sem("gla_scores_read")
        gla_diff, gla_decay, gla_q, gla_k, gla_scores, gla_mixed, gla_out, gla_sq, gla_normed = (
            sem("gla_diff"), sem("gla_decay"), sem("gla_q"), sem("gla_k"), sem("gla_scores"), sem("gla_mixed"),
            sem("gla_out"), sem("gla_sq"), sem("gla_normed"))
        att_qsq, att_rsq, att_qms, att_root, att_diag, att_spread, att_krstd, att_read, att_rep, att_roped = (
            sem("att_qsq"), sem("att_rsq"), sem("att_qms"), sem("att_root"), sem("att_diag"),
            sem("att_spread"), sem("att_krstd"), sem("att_read"),
            sem("att_rep"), sem("att_roped"))
        att_qm, att_scores, att_max, att_exp, att_probs, att_turned, att_pt, att_o, att_done = (
            sem("att_qm"), sem("att_scores"), sem("att_max"), sem("att_exp"),
            sem("att_probs"), sem("att_turned"), sem("att_pt"), sem("att_o"), sem("att_done"))
        sgu_ms, sgu_var, sgu_rstd, sgu_w, sgu_mix, sgu_read, sgu_in = (
            sem("sgu_ms"), sem("sgu_var"), sem("sgu_rstd"), sem("sgu_w"), sem("sgu_mix"),
            sem("sgu_read"), sem("sgu_in"))
        act_chain = Chain(sem("act_chain"))
        dve_chain, pool_chain = Chain(sem("dve_chain")), Chain(sem("pool_chain"))

        def col(name, m, n=1):
            c = COLUMN[name]
            return chan[:, bass.ds(m + c, n)] if not isinstance(m, int) else chan[:, c + m:c + m + n]

        from_xs = lambda turn, k: xs[:, k, :]
        from_inner = lambda turn, k: inner[:, k, :]
        stages = []

        def stage(name, products, turns, signals, count=None, unroll=False):
            s = Stage(name, products, turns)
            s.layer, s.unroll = layer, unroll
            s.counts = {}
            s.signals, s.count = signals, count or turns * len(products)
            stages.append(s)

        for layer in range(2):
            if layer == 0:
                stage("window", [Product(ND, from_xs) for _ in range(4)], NI // 4, "v p")
                stage("pooled", [Product(8, lambda turn, k: inner[:, turn * 8 + k, :])
                                 for _ in range(8)], NI // 8, "")
                stage("silu", [Product(ND, from_xs) for _ in range(4)], NI // 4, "v t q p")
            else:
                stage("conv", [Product(ND, from_xs) for _ in range(4)], NI // 4, "q p")
                lru = []
                for h in range(4):
                    lru += [Product(2, lambda turn, k, h=h: inner[:, turn * 8 + 2 * h + k, :])
                            for _ in range(4)] + [Product(ND, from_xs) for _ in range(2)]
                stage("lru", lru, HEADS // 4, "v t q p", count=NI)
            stage("squared", [Product(NI, from_inner) for _ in range(4)], ND // 4, "p")
            stage("plain", [Product(NP_, from_xs) for _ in range(16)], 1, "")
            stage("gate", [Product(ND, from_xs) for _ in range(4)], ND // 4, "v t q p")
        for layer in (2, 3):
            four = lambda: [Product(ND, from_xs) for _ in range(4)]
            stage("latent", four(), 2, "v t q p", unroll=True)
            stage("rope_k", [Product(ND, from_xs)], 1, "v", unroll=True)
            stage("gqk", four(), 2, "v")
            stage("gv", four(), 2, "v")
            stage("uq", [Product(4, lambda turn, k: latent[:, k, :]) for _ in range(12)], 1, "v",
                  unroll=True)
            stage("ukv", [Product(4, lambda turn, k: latent[:, 4 + k, :]) for _ in range(16)], 1, "v",
                  unroll=True)
            stage("za", four(), 2, "v t q p")
            stage("zc", four(), 2, "v t q p")
            stage("vb", four(), 2, "v t q p", unroll=True)
            stage("ub", four(), 2, "v t q", unroll=True)
            stage("zb", four(), 2, "v t q p")
            mix = []
            for _ in range(4):
                for branch in range(3):
                    mix.append(Product(ND, from_xs))
                    mix.append(Product(8, lambda turn, k, b=branch: y_abc[:, 8 * b + k, :]))
            stage("mix", mix, ND // 4, "v t q p")
            stages[-1].counts = {"v": 3 * ND, "t": 3 * ND, "q": ND, "p": ND}
            stage("wo", [Product(ND, lambda turn, k: merged[:, k, :]) for _ in range(4)], ND // 4, "q")
        COUNTED = {"v": val_ready, "t": act_ready, "q": res_ready, "p": pool_done}
        unit0 = bank0 = 0
        base = dict.fromkeys(COUNTED, 0)
        for s in stages:
            s.unit0, s.bank0, s.base = unit0, bank0, dict(base)
            unit0 += s.turns * s.units
            bank0 += s.turns * s.width
            for c in s.signals.split():
                base[c] += s.counts.get(c, s.count)
            s.end = dict(base)
            s.last_unit = unit0
        n_units = unit0
        assert n_units == weights.shape[0], (n_units, weights.shape)
        norms = {}
        for l in range(2):
            for which in ("enter", "out", "ple", "gate"):
                norms[l, which] = len(norms)
        for l in (2, 3):
            for which in ["enter", "cq", "ckv"] + [f"gla{h}" for h in range(G_HEADS)]:
                norms[l, which] = len(norms)
        ends = {(s.layer, s.name): s.end for s in stages}

        block = ctx.enter_context(nc.Block())

        @block.sync
        def _(sp):
            def load(n, slot):
                if isinstance(n, int) and n >= n_units:
                    return
                wait(sp, lo_done, n - SLOTS + 1)
                sp.dma_start(raw[:, slot, :], weights[n]).then_inc(raw_in[slot], 16)

            sp.dma_start(chan[:], channels).then_inc(consts_in, 16)
            for n in range(LOOKAHEAD):
                load(n, n % SLOTS)

            for s in stages:
                def turn(i):
                    for u in range(s.units):
                        load(i * s.units + (s.unit0 + u + LOOKAHEAD),
                             (s.unit0 + u + LOOKAHEAD) % SLOTS)
                static = 1 if s is stages[-1] else 0
                if s.turns - static > 1:
                    with sp.Fori(0, s.turns - static) as i:
                        turn(i)
                    if static:
                        turn(s.turns - 1)
                else:
                    for i in range(s.turns):
                        turn(i)

        def run_stage(eng, s, turn, per=None, chain=None):
            turn(0)
            if s.unroll:
                for i in range(1, s.turns):
                    turn(i)
                return
            last = 1 if s is stages[-1] else 0
            n = s.turns - 1 - last
            if n > 0:
                with eng.Fori(1, n + 1) as i:
                    if chain is not None:
                        with chain.loop(i - 1, n, per):
                            turn(i)
                    else:
                        turn(i)
            if last:
                turn(s.turns - 1)

        def unit_of(s, i, u):
            return i * s.units + (s.unit0 + u)

        def bank_of(s, i, j):
            return i * s.width + (s.bank0 + j)

        def before(s, i, j):
            return (i, j - 1) if j else (i - 1, s.width - 1)

        @block.tensor
        def _(pe):
            def products(s, i, ready=None, after_first=None):
                tile = 0
                for j, p in enumerate(s.products):
                    bank = banks[:, (s.bank0 + j) % BANKS, :]
                    wait(pe, bank_free, bank_of(s, i, j) - BANKS + 1)
                    for k in range(p.depth):
                        u, c = divmod(p.first_tile + k, UNIT_TILES)
                        slot = (s.unit0 + u) % SLOTS
                        if c == 0:
                            pe.wait_ge(lo_done, unit_of(s, i, u) + 1)
                        if ready is not None and j == 0:
                            ready(k)
                        w = slice(c * P, (c + 1) * P)
                        x = p.operand(i, k)
                        nc.tensor.matmul(bank, w_hi[:, slot, w], x, start=(k == 0), stop=False)
                        ins = nc.tensor.matmul(bank[:, T:2 * T], w_lo[:, slot, w], x[:, 0:T],
                                               start=False, stop=(k == p.depth - 1))
                        if c == UNIT_TILES - 1:
                            ins.then_inc(unit_used, 1)
                    if j == 0 and after_first is not None:
                        after_first()

            def mean_square(l, which, source):
                q = norms[l, which]
                if q:
                    pe.wait_ge(root_ready, q)
                for j, a in enumerate(source):
                    ins = nc.tensor.matmul(ms_bank[:, 0:T], mean_d[:, :], a,
                                           start=(j == 0), stop=(j == len(source) - 1))
                ins.then_inc(ms_ready, 1)

            def mean_square_x(l, which, feed_):
                pe.wait_ge(sq_added, feed_ * 4 + 4)
                mean_square(l, which, act4)

            def turn_tiles(c, use, source):
                for r in range(4):
                    R = (c * 3 + use) * 4 + r
                    wait(pe, turn_read, R - 1)
                    for t in range(4):
                        ins = nc.tensor.transpose(
                            pm[:, r % 2, t * P:(t + 1) * P],
                            source[:, (r % 2) * 4 + t, (r // 2) * P:(r // 2 + 1) * P], tab[:, TABLE["ident"]])
                    ins.then_inc(turned, 1)

            def gla_logits(c):
                pe.wait_ge(small_in, 16 * (c + 1))
                pe.wait_ge(val_ready, ends[c + 2, "rope_k"]["v"])
                wait(pe, sgu_read, c * S_GROUPS)
                for h in range(G_HEADS):
                    ins = nc.tensor.matmul(pm[:, h // 2, (h % 2) * T:(h % 2 + 1) * T],
                                           wa2[:, h * P:(h + 1) * P], ka, start=True, stop=True)
                ins.then_inc(gla_logit, 1)

            def gla_half(c, n):
                h, half = divmod(n, 2)
                N = c * 2 * G_HEADS + n
                pe.wait_ge(gla_q, N + 1)
                pe.wait_ge(gla_k, N + 1)
                wait(pe, gla_scores_read, N)
                if n == 0:
                    pe.wait_ge(turn_read, c * 12 + 4)
                for chunk in range(2):
                    for t in range(4):
                        span = slice(chunk * P, (chunk + 1) * P)
                        if half and t == 3:
                            k_, q_ = gqk[:, 4 + h, span], gqk[:, h, span]
                        else:
                            k_, q_ = g_d[n % 2][:, t, span], g_q[n % 2][:, t, span]
                        ins = nc.tensor.matmul(pm[:, chunk, t * P:(t + 1) * P], k_, q_,
                                               start=True, stop=True)
                if half:
                    ins = nc.tensor.matmul(banks[:, 0, 0:P], g_d[n % 2][:, 3, 0:P],
                                           g_q[n % 2][:, 3, P:2 * P], start=True, stop=True)
                ins.then_inc(gla_scores, 1)

            def gla_output(c, h):
                g = c * G_HEADS + h
                pe.wait_ge(gla_mixed, g + 1)
                wait(pe, gla_normed, g)
                for j in range(2):
                    v0, v1 = (g_v[:, b, h * T + j * P:h * T + (j + 1) * P] for b in range(2))
                    nc.tensor.matmul(pm[:, 2, j * T:j * T + P], v0, g_a[:, 0, :], start=True, stop=True)
                    nc.tensor.matmul(pm[:, 2, j * T + P:(j + 1) * T], v1, g_a[:, 1, :], start=True,
                                     stop=False)
                    ins = nc.tensor.matmul(pm[:, 2, j * T + P:(j + 1) * T], v0, g_a[:, 2, :],
                                           start=False, stop=True)
                ins.then_inc(gla_out, 1)
                pe.wait_ge(gla_sq, g + 1)
                mean_square(c + 2, f"gla{h}", [g_sq[:, 0, :], g_sq[:, 1, :]])

            def gla(c):
                pe.wait_ge(gla_arg, c + 1)
                turn_tiles(c, 0, v_raw)
                for n in range(2 * G_HEADS + 1):
                    if n < 2 * G_HEADS:
                        gla_half(c, n)
                    if n >= 2 and n % 2 == 0:
                        gla_output(c, n // 2 - 1)

            def attention_start(c):
                pe.wait_ge(att_rsq, c + 1)
                pe.wait_ge(gla_normed, (c + 1) * G_HEADS)
                for r in range(4):
                    pe.wait_ge(att_qsq, 4 * c + r + 1)
                    half = r % 2
                    for tb in range(2):
                        tok = slice(tb * P, (tb + 1) * P)
                        at = tb * 8 + half * 4 if r < 2 else 16 + half * 8 + tb * 4
                        rope_sq, rows = ((q_sq[:, 4 + half, tok], tab[:, TABLE["sel"]]) if r < 2 else
                                         (kr_sq[:, tok], tab[:, TABLE["rope_rows"]]))
                        nc.tensor.matmul(pm[:, 2, at:at + 4], rope_sq, rows, start=(r == tb == 0),
                                         stop=False, skip_group_check=True)
                        for h in range(4):
                            ins = nc.tensor.matmul(pm[:, 2, at + h:at + h + 1], q_sq[:, h, tok],
                                                   ones_col, start=False,
                                                   stop=(r == 3 and tb == 1 and h == 3),
                                                   skip_group_check=True)
                    ins.then_inc(att_qms, 1)
                pe.wait_ge(turn_read, c * 12 + 8)
                nc.tensor.matmul(pm[:, 0, 0:T], tab[:, TABLE["rep1"]], ka, start=True, stop=True)
                nc.tensor.matmul(pm[:, 0, T:2 * T], tab[:, TABLE["rep2"]], ka, start=True, stop=True)\
                    .then_inc(att_rep, 1)
                pe.wait_ge(att_roped, c + 1)
                for r in range(2):
                    pe.wait_ge(att_diag, 2 * c + r + 1)
                    wait(pe, att_krstd, 4 * c + 2 * r)
                    for b in range(8):
                        at = (b % 2) * T + (b // 4) * P
                        ins = nc.tensor.matmul(pm[:, (b % 4) // 2, at:at + P], mean_d[:, :], diag[:, b, :],
                                               start=True, stop=True)
                    ins.then_inc(att_spread, 1)

            def attention_scores(c, h):
                g = c * A_HEADS + h
                pe.wait_ge(att_qm, g + 1)
                if h == 0:
                    pe.wait_ge(att_krstd, 4 * (c + 1))
                else:
                    pe.wait_ge(att_read, g)
                q_rope = qm[h % 2]
                for tb in range(2):
                    keys = slice(0, (tb + 1) * P)
                    o_ = pm[:, 0, 0:P] if tb == 0 else pm[:, 0, P:3 * P]
                    tok = slice(tb * P, (tb + 1) * P)
                    nc.tensor.matmul(o_, q_buf[:, h, tok], k_buf[:, h, keys], start=True, stop=False)
                    nc.tensor.matmul(o_, q_rope[:, 0, tok], kr[:, 0, keys], start=False, stop=False)
                    ins = nc.tensor.matmul(o_, q_rope[:, 1, tok], kr[:, 1, keys], start=False, stop=True)
                ins.then_inc(att_scores, 1)

            def attention_turn(c, h):
                g = c * A_HEADS + h
                pe.wait_ge(att_probs, g + 1)
                wait(pe, att_pt, g)
                for t in range(3):
                    ins = nc.tensor.transpose(pm[:, 1, t * P:(t + 1) * P],
                                              probs[h % 2][:, t * P:(t + 1) * P],
                                              tab[:, TABLE["ident"]])
                ins.then_inc(att_turned, 1)

            def attention_output(c, h):
                g = c * A_HEADS + h
                pe.wait_ge(att_pt, g + 1)
                wait(pe, att_done, g)
                v0, v1 = (a_v[:, b, h * P:(h + 1) * P] for b in range(2))
                nc.tensor.matmul(pm[:, 2, 0:P], v0, probs_t[:, 0:P], start=True, stop=True)
                nc.tensor.matmul(pm[:, 2, P:T], v0, probs_t[:, P:2 * P], start=True, stop=False)
                nc.tensor.matmul(pm[:, 2, P:T], v1, probs_t[:, 2 * P:3 * P], start=False, stop=True)\
                    .then_inc(att_o, 1)

            def attention(c):
                turn_tiles(c, 1, v_raw)
                attention_start(c)
                attention_scores(c, 0)
                for h in range(A_HEADS):
                    if h < A_HEADS - 1:
                        attention_scores(c, h + 1)
                    if h:
                        attention_output(c, h - 1)
                    attention_turn(c, h)
                attention_output(c, A_HEADS - 1)

            def spatial_gate(c):
                pe.wait_ge(pool_done, ends[c + 2, "vb"]["p"])
                pe.wait_ge(att_done, (c + 1) * A_HEADS)
                for tb in range(2):
                    ins = nc.tensor.matmul(pm[:, 2, tb:tb + 1], acc[:, tb * P:(tb + 1) * P],
                                           mean_d[:, 0:1], start=(tb == 0), stop=(tb == 1),
                                           skip_group_check=True)
                ins.then_inc(sgu_ms, 1)
                turn_tiles(c, 2, s_v)
                pe.wait_ge(sgu_w, c + 1)
                pe.wait_ge(turn_read, c * 12 + 12)
                for g in range(S_GROUPS):
                    r = c * S_GROUPS + g
                    if g >= 2:
                        pe.wait_ge(sgu_read, r - 1)
                    for chunk in range(2):
                        ins = nc.tensor.matmul(pm[:, g % 2, chunk * P:(chunk + 1) * P],
                                               s_vt[:, chunk, g * P:(g + 1) * P], w_st[:, g, :],
                                               start=True, stop=True)
                    ins.then_inc(sgu_mix, 1)

            act4 = [act[:, j, :] for j in range(4)]
            pe.wait_ge(consts_ready, 1)
            feeds = 0
            for n, s in enumerate(stages):
                l = s.layer
                ready = hook = None
                if s.name in ("window", "conv", "latent"):
                    ready = lambda k, f=feeds: pe.wait_ge(xs_ready, f * ND + k + 1)
                    hook = lambda f=feeds: mean_square_x(l, "enter", f)
                    feeds += 1
                elif s.name == "gate":
                    ready = lambda k, f=feeds: pe.wait_ge(xs_ready, f * ND + k + 1)
                    hook = lambda f=feeds: mean_square_x(l, "ple", f)
                    feeds += 1
                elif s.name == "squared":
                    ready = lambda k, b=stages[n - 1].base["p"]: pe.wait_ge(pool_done, b + k + 1)
                elif s.name == "plain":
                    ready = lambda k: pe.wait_ge(p_ready, l * NP_ + k + 1)
                elif s.name == "wo":
                    ready = lambda k, b=stages[n - 1].base["p"]: pe.wait_ge(pool_done, b + k + 1)
                if s.name in ("lru", "mix"):
                    pe.wait_ge(pool_done, s.base["p"])
                if s.name in ("uq", "ukv"):
                    pe.wait_ge(res_ready, ends[l, "latent"]["q"])

                def turn(i):
                    if s.name == "pooled":
                        pe.wait_ge(tile_split, i * 8 + 8)
                    static = isinstance(i, int) and i == 0
                    products(s, i, ready if static else None, hook if static else None)
                run_stage(pe, s, turn)
                if s.name in ("plain", "gate"):
                    pe.wait_ge(pool_done, s.end["p"])
                    mean_square(l, "out" if s.name == "plain" else "gate", [acc[:, :]])
                if s.name == "rope_k":
                    pe.wait_ge(pool_done, s.base["p"])
                    mean_square(l, "cq", [acc[:, :]])
                    mean_square(l, "ckv", [acc_kv[:, :]])
                if s.name == "gqk":
                    gla_logits(l - 2)
                if s.name == "gv":
                    pe.wait_ge(val_ready, s.end["v"])
                    pe.wait_ge(tables_in, 16)
                    gla(l - 2)
                if s.name == "ukv":
                    pe.wait_ge(val_ready, s.end["v"])
                    attention(l - 2)
                if s.name == "vb":
                    spatial_gate(l - 2)

        @block.scalar
        def _(sc):
            def split_hi(n, slot):
                if isinstance(n, int) and n >= n_units:
                    return
                sc.wait_ge(raw_in[slot], (n - slot) * 4 + 16)
                wait(sc, unit_used, n - SLOTS + 1)
                nc.scalar.activation(w_hi[:, slot, :], raw[:, slot, :], ACT.Copy).then_inc(hi_done, 1)

            def read_small(s, i, j):
                b = (s.bank0 + j) % BANKS
                sc.wait_ge(unit_used, unit_of(s, i, s.products[j].last_unit) + 1)
                wait(sc, bank_free, bank_of(s, i, j) - 1)
                nc.scalar.activation(small[:, b % 2, :], banks[:, b, T:2 * T], ACT.Copy)\
                    .then_inc(small_ready, 1)

            def feed(f, gain, first):
                for b in range(4):
                    if first:
                        if b == 0:
                            sc.wait_ge(x_loaded, 16)
                            sc.wait_ge(consts_in, 16)
                    elif f == 5:
                        sc.wait_ge(res_ready, ends[2, "wo"]["q"])
                    else:
                        sc.wait_ge(x_updated, (f - 1) * 4 + b + 1)
                    for k in range(4 * b, 4 * b + 4):
                        nc.scalar.activation(xs[:, k, 0:T], x_buf[:, k, :], ACT.Copy,
                                             scale=col(gain, k)).then_inc(x_hi, 1)
                    wait(sc, sq_added, f * 4 + b)
                    nc.scalar.activation(val[:, :, :], x_buf[:, 4 * b:4 * b + 4, :], ACT.Square)\
                        .then_inc(x_sq, 1)

            def root(l, which, width=D):
                q = norms[l, which]
                sc.wait_ge(ms_ready, q + 1)
                wait(sc, rstd_ready, q)
                nc.scalar.activation(rms[:], ms_bank[:, 0:T], ACT.Sqrt, scale=D / width,
                                     bias=eps_col).then_inc(root_ready, 1)

            def rope_tables():
                sc.wait_ge(rope_arg, 1)
                nc.scalar.activation(rope_sin[:], sq[:], ACT.Sin).then_inc(rope_done, 1)
                nc.scalar.activation(rope_cos[:], acc_kv[:], ACT.Sin).then_inc(rope_done, 1)

            def read_turned(c, use, dest, scale=None):
                for r in range(4):
                    R = (c * 3 + use) * 4 + r
                    sc.wait_ge(turned, R + 1)
                    d = dest[:, r // 2, (r % 2) * 512:(r % 2 + 1) * 512]
                    if scale is None:
                        ins = nc.scalar.activation(d, pm[:, r % 2, :], ACT.Copy)
                    else:
                        ins = nc.scalar.activation(d, pm[:, r % 2, :], ACT.Copy,
                                                   scale=scale[:, r // 2:r // 2 + 1])
                    ins.then_inc(turn_read, 1)

            def gla_forget(c):
                sc.wait_ge(gla_arg, c + 1)
                act_chain.link(sc, nc.scalar.activation(g_e, g_x, ACT.Abs))
                act_chain.link(sc, nc.scalar.activation(g_e, g_e, ACT.Exp, scale=-1.0))
                nc.scalar.activation(g_e, g_e, ACT.Ln, bias=ones_col).then_inc(gla_exp, 1)

            def gla(c):
                read_turned(c, 0, g_v)

                def decay(n):
                    N = c * 2 * G_HEADS + n
                    d = g_d[n % 2]
                    sc.wait_ge(gla_diff, N + 1)
                    act_chain.link(sc, nc.scalar.activation(d, d, ACT.Abs))
                    nc.scalar.activation(d, d, ACT.Exp, scale=-1.0).then_inc(gla_decay, 1)

                decay(0)
                for n in range(2 * G_HEADS + 1):
                    if n < 2 * G_HEADS - 1:
                        decay(n + 1)
                    if n >= 2 and n % 2 == 0:
                        h = n // 2 - 1
                        sc.wait_ge(gla_out, c * G_HEADS + h + 1)
                        nc.scalar.activation(g_sq.rearrange("p a b -> p (a b)"), pm[:, 2, :],
                                             ACT.Square).then_inc(gla_sq, 1)
                        root(c + 2, f"gla{h}", 2 * P)

            def attention(c):
                read_turned(c, 1, a_v)
                for r in range(4):
                    wait(sc, att_qms, 4 * c + r)
                    source = (q_buf if r < 2 else k_buf)[:, 4 * (r % 2):4 * (r % 2) + 4, :]
                    nc.scalar.activation(q_sq[:, 0:4, :], source, ACT.Square).then_inc(att_qsq, 1)
                sc.wait_ge(att_qms, 4 * c + 4)
                nc.scalar.activation(rms_cols, pm[:, 2, 0:32], ACT.Sqrt, scale=1.0 / QK, bias=eps_col)\
                    .then_inc(att_root, 1)
                for r in range(2):
                    sc.wait_ge(att_spread, 2 * c + r + 1)
                    for b in range(2):
                        at = 4 * r + 2 * b
                        nc.scalar.activation(k_rstd[:, at:at + 2, :].rearrange("p a b -> p (a b)"),
                                             pm[:, b, :], ACT.Copy, scale=float(D)).then_inc(att_krstd, 1)

                def copy_out(h):
                    sc.wait_ge(att_o, c * A_HEADS + h + 1)
                    nc.scalar.activation(q_buf[:, h, :], pm[:, 2, 0:T], ACT.Copy).then_inc(att_done, 1)

                for h in range(A_HEADS + 2):
                    g = c * A_HEADS + h
                    if h < A_HEADS:
                        sc.wait_ge(att_max, g + 1)
                        for tb in range(2):
                            span = slice(0, P) if tb == 0 else slice(P, 3 * P)
                            nc.scalar.activation(probs[h % 2][:, span], att_s[h % 2][:, span], ACT.Exp,
                                                 scale=q_scale[:, tb * 8 + h:tb * 8 + h + 1],
                                                 bias=s_bias[:, h % 2, tb:tb + 1],
                                                 accum_out=s_sum[:, h % 2, tb:tb + 1])\
                                .then_inc(att_exp, 1)
                    if h >= 2:
                        copy_out(h - 2)
                    if 1 <= h <= A_HEADS:
                        sc.wait_ge(att_turned, g)
                        nc.scalar.activation(probs_t, pm[:, 1, 0:3 * P], ACT.Copy).then_inc(att_pt, 1)

            def spatial_gate(c):
                sc.wait_ge(sgu_rstd, c + 1)
                read_turned(c, 2, s_vt, s_rstd)

            sc.dma_start(x_buf, x_in).then_inc(x_loaded, 16)
            sc.dma_start(inv_count[:], inv_counts).then_inc(consts_in, 16)
            for n in range(LOOKAHEAD):
                split_hi(n, n % SLOTS)
            sc.wait_ge(consts_in, 32)
            nc.scalar.activation(tiny[:, 1, :], col("lru_L", 0, NI), ACT.Abs).then_inc(decay_e, 1)
            sc.wait_ge(decay_e, 1)
            nc.scalar.activation(tiny[:, 0, :], tiny[:, 1, :], ACT.Exp, scale=-1.0).then_inc(decay_e, 1)
            feeds = gelus = 0
            for n, s in enumerate(stages):
                l = s.layer
                if s.name in ("window", "conv"):
                    if l:
                        root(0, "gate")
                    feed(feeds, f"g_pre{l}", feeds == 0)
                    if feeds:
                        sc.dma_start(x_scratch, x_buf).then_inc(x_saved, 16)
                    feeds += 1
                if s.name == "squared":
                    sc.wait_ge(res_ready, s.base["q"])
                    sc.dma_start(x_buf, x_scratch if l else x_in).then_inc(x_loaded, 16)
                    sc.dma_start(p_raw[:], p_in[l]).then_inc(p_loaded, 16)
                    sc.wait_ge(p_loaded, 16 * (l + 1))
                    sc.wait_ge(unit_used, s.unit0)
                    nc.scalar.activation(xs[:, 0:NP_, 0:T], p_raw[:], ACT.Copy).then_inc(p_hi, 1)
                if s.name == "gate":
                    root(l, "out")
                    feed(feeds, f"g_ple_in{l}", False)
                    feeds += 1
                if s.name == "latent":
                    if l == 2:
                        root(1, "gate")
                    feed(feeds, f"norm_g{l - 2}", False)
                    feeds += 1
                    if l == 2:
                        sc.dma_start(tab[:], tables).then_inc(tables_in, 16)
                        sc.dma_start(pos_int[:], positions).then_inc(pos_ready, 16)
                        rope_tables()
                if s.name == "rope_k":
                    sc.wait_ge(unit_used, s.unit0)
                    sc.dma_start(wa2, w_a2[l - 2]).then_inc(small_in, 16)
                if s.name == "vb":
                    sc.wait_ge(res_ready, s.base["q"])
                    sc.dma_start(w_st, w_s[l - 2]).then_inc(sgu_in, 16)
                    sc.dma_start(b_st, b_s[l - 2]).then_inc(sgu_in, 16)

                def head(i, h):
                    m = i * 8 + 2 * h
                    t = i * 4 + h
                    for j in range(4):
                        sc.wait_ge(bank_free, bank_of(s, i, 6 * h + j) + 1)
                        if j == 0:
                            wait(sc, lru_y, t)
                        nc.scalar.activation(lru_act[:, j, :], val[:, j, :], ACT.Tanh, scale=0.5,
                                             bias=half_b[:, j // 2, bass.ds(m + j % 2, 1)]
                                             if not isinstance(m, int) else
                                             half_b[:, j // 2, m + j % 2:m + j % 2 + 1])\
                            .then_inc(lru_sig, 1)

                def head_decay(i, h):
                    t = i * 4 + h
                    sc.wait_ge(lru_p, t + 1)
                    nc.scalar.activation(lru_a[:, :, :], val[:, 0:2, :], ACT.Exp, scale=-1.0)\
                        .then_inc(lru_at, 1)
                    nc.scalar.activation(lru_act[:, 0:2, :], val[:, 0:2, :], ACT.Tanh)\
                        .then_inc(lru_at, 1)

                def head_root(i, h):
                    t = i * 4 + h
                    sc.wait_ge(lru_m, t + 1)
                    nc.scalar.activation(lru_act[:, 0:2, :], lru_act[:, 0:2, :], ACT.Sqrt)\
                        .then_inc(lru_root, 1)

                def turn(i):
                    for u in range(s.units):
                        n_ = s.unit0 + u + LOOKAHEAD
                        split_hi(i * s.units + n_, n_ % SLOTS)
                        if s.name == "lru":
                            h, q = divmod(u, 5)
                            if q == 1:
                                if not (isinstance(i, int) and i == h == 0):
                                    tanh_z(*((i, h - 1) if h else (i - 1, 3)), 1)
                                head(i, h)
                            elif q == 2:
                                head_decay(i, h)
                            elif q == 3:
                                tanh_z(i, h, 0)
                                head_root(i, h)
                        for j, p in enumerate(s.products):
                            if p.last_unit != u:
                                continue
                            read_small(s, i, j)
                            if (s.name in ("window", "conv", "latent", "gate")
                                    and isinstance(i, int) and i == j == 0):
                                root(l, "ple" if s.name == "gate" else "enter")
                            m = i * s.width + j
                            if s.name == "latent":
                                sc.wait_ge(val_ready, m + s.base["v"] + 1)
                                nc.scalar.activation(latent[:, m, 0:T], val[:, j % 4, :], ACT.Copy,
                                                     scale=col(("cq_g%d" if m < 4 else "ckv_g%d")
                                                               % (l - 2), m % 4)).then_inc(act_ready, 1)
                            if s.name in ("vb", "ub") and m:
                                gelu_tanh(m - 1)
                            if s.name == "mix" and j % 2 == 0:
                                pair = i * (s.width // 2) + j // 2
                                slot = (j // 2) % 2
                                sc.wait_ge(val_ready, pair + (s.base["v"] + 1))
                                nc.scalar.activation(act[:, slot, :], val[:, 2 * slot, :], ACT.Tanh,
                                                     scale=0.5).then_inc(act_ready, 1)
                            if s.name in ("silu", "gate", "za", "zc", "zb"):
                                sc.wait_ge(val_ready, m + (s.base["v"] + 1))
                                wait(sc, pool_done, m + (s.base["p"] - 3))
                                nc.scalar.activation(act[:, j % 4, :], val[:, j % 4, :], ACT.Tanh,
                                                     scale=0.5).then_inc(act_ready, 1)

                def tanh_z(i, h, j):
                    z = i * 8 + 2 * h + j
                    sc.wait_ge(val_ready, z + (s.base["v"] + 1))
                    wait(sc, pool_done, z + (s.base["p"] - 1))
                    nc.scalar.activation(act[:, j, :], act[:, 2 + j, :], ACT.Tanh, scale=0.5)\
                        .then_inc(act_ready, 1)

                def gelu_tanh(m):
                    sc.wait_ge(inner_ready, gelus * 8 + m + 1)
                    a = act[:, m % 4, :]
                    nc.scalar.activation(a, a, ACT.Tanh, scale=GELU_A).then_inc(act_ready, 1)

                run_stage(sc, s, turn)
                if s.name == "lru":
                    tanh_z(s.turns - 1, 3, 1)
                if s.name in ("vb", "ub"):
                    gelu_tanh(7)
                    gelus += 1
                if s.name == "rope_k":
                    root(l, "cq", RANK)
                    root(l, "ckv", RANK)
                if s.name == "gqk":
                    gla_forget(l - 2)
                if s.name == "gv":
                    gla(l - 2)
                if s.name == "ukv":
                    attention(l - 2)
                if s.name == "vb":
                    spatial_gate(l - 2)
            sc.wait_ge(res_ready, stages[-1].end["q"])
            sc.dma_start(out, x_buf).then_inc(out_done, 16)
            sc.wait_ge(out_done, 16)

        @block.vector
        def _(ve):
            link = lambda ins: dve_chain.link(ve, ins)

            def split_lo(n, slot):
                if isinstance(n, int) and n >= n_units:
                    return
                ve.wait_ge(hi_done, n + 1)
                nc.vector.tensor_tensor(w_lo[:, slot, :], raw[:, slot, :], w_hi[:, slot, :].bitcast(F32),
                                        ALU.subtract).then_inc(lo_done, 1)

            def read_bank(s, i, j, out_):
                b = (s.bank0 + j) % BANKS
                ve.wait_ge(small_ready, bank_of(s, i, j) + 1)
                ins = nc.vector.tensor_tensor(out_, banks[:, b, 0:T], small[:, b % 2, :], ALU.add)
                ins.then_inc(bank_free, 1)
                ve.wait_ge(bank_free, bank_of(s, i, j) + 1)
                return ins

            def norm(l, which, dest):
                q = norms[l, which]
                ve.wait_ge(root_ready, q + 1)
                nc.vector.reciprocal(dest[:, 0:T], rms[:]).then_inc(rstd_ready, 1)
                ve.wait_ge(rstd_ready, q + 1)

            def feed(f, gain, residual):
                if residual is not None:
                    source, res_gain, l, which = residual
                    norm(l, which, rstd_r)

                def lows(b):
                    for k in range(4 * b, 4 * b + 4):
                        ve.wait_ge(x_hi, f * ND + k + 1)
                        nc.vector.scalar_tensor_tensor(
                            out=xs[:, k, T:2 * T], in0=x_buf[:, k, :], scalar=col(gain, k),
                            in1=xs[:, k, 0:T].bitcast(F32), op0=ALU.mult, op1=ALU.subtract)\
                            .then_inc(xs_ready, 1)
                for b in range(4):
                    if residual is not None:
                        r4 = source[:, 4 * b:4 * b + 4, :]
                        link(nc.vector.tensor_tensor(
                            r4, r4, rstd_r[:, None, :].broadcast_to([P, 4, T]), ALU.mult))
                        for k in range(4 * b, 4 * b + 4):
                            ins = nc.vector.scalar_tensor_tensor(
                                out=x_buf[:, k, :], in0=source[:, k, :], scalar=col(res_gain, k),
                                in1=x_buf[:, k, :], op0=ALU.mult, op1=ALU.add)
                        ins.then_inc(x_updated, 1)
                    if gain is not None and b:
                        lows(b - 1)
                if gain is not None:
                    lows(3)

            def log1p_over_2(s_, s2, t_):
                link(nc.vector.tensor_tensor(s2, s_, s_, ALU.mult))
                link(nc.vector.tensor_scalar(t_, s2, 1.0 / 15, None, ALU.mult))
                for c in (13, 11, 9, 7, 5, 3):
                    link(nc.vector.scalar_tensor_tensor(out=t_, in0=t_, scalar=1.0 / c, in1=s2,
                                                        op0=ALU.add, op1=ALU.mult))
                link(nc.vector.scalar_tensor_tensor(out=t_, in0=t_, scalar=1.0, in1=s_,
                                                    op0=ALU.add, op1=ALU.mult))

            def flat(a):
                return a.rearrange("p a b -> p (a b)")

            def rope_angles():
                ve.wait_ge(pos_ready, 16)
                ve.wait_ge(tables_in, 16)
                ang, n_ = sq[:], acc_kv[:]
                link(nc.vector.tensor_copy(n_, pos_int[:]))
                link(nc.vector.tensor_scalar(ang, n_, tab[:, TABLE["inv_freq"]], None, ALU.mult))
                magic = 1.5 * 2.0 ** 23
                link(nc.vector.tensor_scalar(n_, ang, 1.0 / (2 * np.pi), magic, ALU.mult, ALU.add))
                link(nc.vector.tensor_scalar(n_, n_, magic, None, ALU.subtract))
                for part in TWO_PI:
                    link(nc.vector.scalar_tensor_tensor(out=ang, in0=n_, scalar=-part, in1=ang,
                                                        op0=ALU.mult, op1=ALU.add))
                pi = float(np.nextafter(np.float32(np.pi), np.float32(0)))
                link(nc.vector.tensor_scalar(ang, ang, pi, -pi, ALU.min, ALU.max))
                link(nc.vector.tensor_scalar(n_, ang, -1.0, None, ALU.mult))
                link(nc.vector.tensor_tensor(n_, ang, n_, ALU.max))
                nc.vector.tensor_scalar(n_, n_, -1.0, float(np.pi / 2), ALU.mult, ALU.add)\
                    .then_inc(rope_arg, 1)
                ve.wait_ge(rope_done, 2)

            def gla_bias(c):
                ve.wait_ge(gla_logit, c + 1)
                for h in range(G_HEADS):
                    ins = nc.vector.tensor_scalar(g_x[:, h, :], pm[:, h // 2, (h % 2) * T:(h % 2 + 1) * T],
                                                  col(f"b_a{c}", h), None, ALU.add)
                ins.then_inc(gla_arg, 1)

            def gla(c):
                ve.wait_ge(gla_arg, c + 1)
                x_, e_ = flat(g_x), flat(g_e)
                ve.wait_ge(gla_exp, c + 1)
                link(nc.vector.tensor_scalar(x_, x_, 0.0, 1.0 / G_TAU, ALU.min, ALU.mult))
                link(nc.vector.scalar_tensor_tensor(out=x_, in0=e_, scalar=-1.0 / G_TAU, in1=x_,
                                                    op0=ALU.mult, op1=ALU.add))
                for h in range(G_HEADS):
                    ins = nc.vector.tensor_tensor_scan(
                        out=b_cum[:, h, :], data0=power[:, 2:3].broadcast_to([P, T]),
                        data1=g_x[:, h, :], initial=0.0, op0=ALU.mult, op1=ALU.add)
                link(ins)
                masks = tab[:, TABLE["masks"]].rearrange("p (l t) -> p l t", t=P)
                halves = 2 * G_HEADS

                def difference(n):
                    h, half = divmod(n, 2)
                    b_ = b_cum[:, h, :]
                    for t in range(4):
                        span = 2 << (4 * half + t)
                        by_span = b_.rearrange("p (n s) -> p n s", s=span)
                        mid = by_span[:, :, span // 2 - 1:span // 2]
                        ins = nc.vector.tensor_tensor(
                            g_d[n % 2][:, t, :].rearrange("p (n s) -> p n s", s=span), by_span,
                            mid.broadcast_to([P, T // span, span]), ALU.subtract)
                    ins.then_inc(gla_diff, 1)

                def mask(n):
                    h, half = divmod(n, 2)
                    N = c * halves + n
                    ve.wait_ge(gla_scores, N + 1)
                    wait(ve, gla_mixed, c * G_HEADS + h)
                    if half:
                        wait(ve, gla_out, c * G_HEADS + h)
                        nc.vector.tensor_scalar(g_a[:, 2, :], banks[:, 0, 0:P], G_DK ** -0.5, None,
                                                ALU.mult)
                    for chunk in range(2):
                        ins = nc.vector.tensor_tensor(
                            g_m[chunk][:, 4 * half:4 * half + 4, :],
                            pm[:, chunk, :].rearrange("p (l t) -> p l t", t=P),
                            masks[:, 4 * half:4 * half + 4, :], ALU.mult)
                    ins.then_inc(gla_scores_read, 1)

                difference(0)
                for n in range(halves + 2):
                    N = c * halves + n
                    if n < halves:
                        h = n // 2
                        ve.wait_ge(gla_decay, N + 1)
                        nc.vector.tensor_tensor(g_q[n % 2], g_d[n % 2],
                                                gqk[:, h:h + 1, :].broadcast_to([P, 4, T]), ALU.mult)\
                            .then_inc(gla_q, 1)
                    if 1 <= n <= halves:
                        mask(n - 1)
                    if n < halves - 1:
                        difference(n + 1)
                    if n >= 2 and n % 2 == 0:
                        ve.wait_ge(gla_scores_read, N)
                        for chunk in range(2):
                            ins = nc.vector.tensor_reduce(g_a[:, chunk, :],
                                                          g_m[chunk].rearrange("p l t -> p t l"),
                                                          mybir.AxisListType.X, ALU.add)
                        ins.then_inc(gla_mixed, 1)
                    if n >= 3 and n % 2:
                        h = (n - 3) // 2
                        norm(c + 2, f"gla{h}", g_rstd)
                        for j in range(2):
                            ins = nc.vector.scalar_tensor_tensor(
                                out=g_o[:, 2 * h + j, :], in0=pm[:, 2, j * T:(j + 1) * T],
                                scalar=col(f"o_g{c}", j), in1=g_rstd, op0=ALU.mult, op1=ALU.mult)
                        ins.then_inc(gla_normed, 1)

            def rotate(x1, x2, t1, t2, cos, sin):
                nc.vector.tensor_tensor(t1, x1, sin, ALU.mult)
                link(nc.vector.tensor_tensor(t2, x2, sin, ALU.mult))
                link(nc.vector.tensor_tensor(x1, x1, cos, ALU.mult))
                nc.vector.tensor_tensor(x1, x1, t2, ALU.subtract)
                link(nc.vector.tensor_tensor(x2, x2, cos, ALU.mult))
                return nc.vector.tensor_tensor(x2, x2, t1, ALU.add)

            def attention(c):
                x1, x2 = q_buf[:, 8:12:2, :], q_buf[:, 9:12:2, :]
                nc.vector.tensor_tensor(kr_sq, ka, ka, ALU.mult)
                nc.vector.tensor_tensor(r1, x1, x1, ALU.mult)
                link(nc.vector.tensor_tensor(r2, x2, x2, ALU.mult))
                ins = nc.vector.tensor_tensor(q_sq[:, 4:6, :], r1, r2, ALU.add)
                ins.then_inc(att_rsq, 1)
                ve.wait_ge(att_rsq, c + 1)
                ve.wait_ge(att_qms, 4 * c + 2)
                nc.vector.tensor_scalar(q_buf[:, 0:8, :], q_buf[:, 0:8, :], col(f"gq_nope{c}", 0),
                                        col(f"gk_nope{c}", 0), ALU.mult, ALU.mult)
                nc.vector.tensor_scalar(x1, x1, col(f"gq_r1{c}", 0), None, ALU.mult)
                link(nc.vector.tensor_scalar(x2, x2, col(f"gq_r2{c}", 0), None, ALU.mult))
                cos2, sin2 = (t[:, None, :].broadcast_to([P, 2, T]) for t in (rope_cos[:], rope_sin[:]))
                link(rotate(x1, x2, r1, r2, cos2, sin2))
                ve.wait_ge(att_rep, c + 1)
                nc.vector.tensor_scalar(kr[:, 0, :], pm[:, 0, 0:T], col(f"gk_r1{c}", 0), None, ALU.mult)
                link(nc.vector.tensor_scalar(kr[:, 1, :], pm[:, 0, T:2 * T], col(f"gk_r2{c}", 0), None,
                                             ALU.mult))
                rotate(kr[:, 0, :], kr[:, 1, :], r1[:, 0, :], r2[:, 0, :], rope_cos[:], rope_sin[:])\
                    .then_inc(att_roped, 1)
                ve.wait_ge(att_root, c + 1)
                link(nc.vector.reciprocal(rstd_cols, rms_cols))
                link(nc.vector.tensor_scalar(q_scale, rstd_cols[:, 0:16], QK ** -0.5, None, ALU.mult))
                for r in range(2):
                    wait(ve, att_spread, 2 * c + r)
                    nc.vector.tensor_tensor(
                        diag, tab[:, None, TABLE["ident"]].broadcast_to([P, 8, P]),
                        rstd_cols[:, 16 + 8 * r:24 + 8 * r, None].broadcast_to([P, 8, P]),
                        ALU.mult).then_inc(att_diag, 1)
                neg = tab[:, TABLE["neg"]]
                ve.wait_ge(att_krstd, 4 * (c + 1))

                def softmax_start(h):
                    g, s_, slot = c * A_HEADS + h, att_s[h % 2], h % 2
                    ve.wait_ge(att_scores, g + 1)
                    nc.vector.tensor_tensor(s_[:, 0:P], pm[:, 0, 0:P], k_rstd[:, h, 0:P], ALU.mult)
                    nc.vector.tensor_tensor(s_[:, P:3 * P], pm[:, 0, P:3 * P], k_rstd[:, h, :],
                                            ALU.mult).then_inc(att_read, 1)
                    ve.wait_ge(att_read, g + 1)
                    blocks = s_.rearrange("p (b k) -> p b k", k=P)[:, 0:3:2, :]
                    link(nc.vector.tensor_tensor(blocks, blocks, neg[:, None, :].broadcast_to([P, 2, P]),
                                                 ALU.add))
                    nc.vector.tensor_reduce(s_max[:, slot, 0:1], s_[:, 0:P], mybir.AxisListType.X,
                                            ALU.max)
                    link(nc.vector.tensor_reduce(s_max[:, slot, 1:2], s_[:, P:3 * P],
                                                 mybir.AxisListType.X, ALU.max))
                    for tb in range(2):
                        ins = nc.vector.scalar_tensor_tensor(
                            out=s_bias[:, slot, tb:tb + 1], in0=s_max[:, slot, tb:tb + 1], scalar=-1.0,
                            in1=q_scale[:, tb * 8 + h:tb * 8 + h + 1], op0=ALU.mult, op1=ALU.mult)
                    ins.then_inc(att_max, 1)

                def softmax_end(h):
                    g, p_, slot = c * A_HEADS + h, probs[h % 2], h % 2
                    ve.wait_ge(att_exp, 2 * g + 2)
                    link(nc.vector.reciprocal(s_inv[:, slot, :], s_sum[:, slot, :]))
                    nc.vector.tensor_scalar(p_[:, 0:P], p_[:, 0:P], s_inv[:, slot, 0:1], None, ALU.mult)
                    nc.vector.tensor_scalar(p_[:, P:3 * P], p_[:, P:3 * P], s_inv[:, slot, 1:2], None,
                                            ALU.mult).then_inc(att_probs, 1)

                for h in range(A_HEADS):
                    softmax_start(h)
                    if h:
                        softmax_end(h - 1)
                softmax_end(A_HEADS - 1)

            def spatial_gate(c):
                ve.wait_ge(sgu_ms, c + 1)
                nc.vector.tensor_scalar(s_col, pm[:, 2, 0:2], D / 1024, EPS, ALU.mult, ALU.add)\
                    .then_inc(sgu_var, 1)
                ve.wait_ge(sgu_in, 32 * (c + 1))
                nc.vector.tensor_tensor(w_st, w_st, tab[:, None, TABLE["tri"]].broadcast_to(
                    [P, S_GROUPS, P]), ALU.mult).then_inc(sgu_w, 1)
                for g in range(S_GROUPS):
                    ve.wait_ge(sgu_mix, c * S_GROUPS + g + 1)
                    nc.vector.scalar_tensor_tensor(
                        out=s_mix[:, g, :].rearrange("p (c t) -> p c t", t=P),
                        in0=pm[:, g % 2, 0:T].rearrange("p (c t) -> p c t", t=P),
                        scalar=col(f"v_g{c}", g), in1=b_st[:, g:g + 1, :].broadcast_to([P, 2, P]),
                        op0=ALU.mult, op1=ALU.add).then_inc(sgu_read, 1)
                ve.wait_ge(sgu_read, (c + 1) * S_GROUPS)

            nc.vector.memset(mean_d[:], 1.0 / D)
            nc.vector.memset(power[:, 0:1], -0.5)
            nc.vector.memset(power[:, 2:3], 1.0)
            nc.vector.memset(power[:, 3:4], EPS)
            nc.vector.memset(taps_in[:], 0.0)
            nc.vector.memset(acc[:], 0.0)
            link(nc.vector.memset(win[:], 0.0))
            nc.vector.tensor_copy(rms[:, 0:1], win[:, 0, 0:1]).then_inc(consts_ready, 1)
            ve.wait_ge(consts_in, 32)
            nc.vector.tensor_scalar(half_b[:, 0, :], col("lru_ba", 0, NI), 0.5, None, ALU.mult)
            nc.vector.tensor_scalar(half_b[:, 1, :], col("lru_bx", 0, NI), 0.5, None, ALU.mult)\
                .then_inc(consts_ready, 1)
            for n in range(LOOKAHEAD):
                split_lo(n, n % SLOTS)
            ve.wait_ge(decay_e, 2)
            e, s2, s_, t_ = (tiny[:, j, :] for j in range(4))
            link(nc.vector.tensor_scalar(t_, e, 2.0, None, ALU.add))
            link(nc.vector.reciprocal(t_, t_))
            link(nc.vector.tensor_tensor(s_, e, t_, ALU.mult))
            log1p_over_2(s_, s2, t_)
            link(nc.vector.tensor_scalar(s_, col("lru_L", 0, NI), -LRU_C, 0.0, ALU.mult, ALU.max))
            link(nc.vector.scalar_tensor_tensor(out=decay[:], in0=t_, scalar=2 * LRU_C, in1=s_,
                                                op0=ALU.mult, op1=ALU.add))

            feeds = gelus = 0
            for n, s in enumerate(stages):
                l = s.layer
                if s.name == "za":
                    ve.wait_ge(att_done, (l - 1) * A_HEADS)
                if n:
                    wait(ve, pool_done, s.base["p"])
                if s.name in ("window", "conv"):
                    feed(feeds, f"g_pre{l}", (gated, "g_ple_out0", 0, "gate") if l else None)
                    feeds += 1
                if s.name == "conv":
                    ve.wait_ge(x_saved, 16)
                if s.name == "latent":
                    feed(feeds, f"norm_g{l - 2}", (gated, "g_ple_out1", 1, "gate") if l == 2 else None)
                    feeds += 1
                    if l == 2:
                        rope_angles()
                if s.name == "squared":
                    ve.wait_ge(x_loaded, 16 * (2 + l))
                    ve.wait_ge(p_hi, l + 1)
                    for k in range(NP_):
                        nc.vector.tensor_tensor(xs[:, k, T:2 * T], p_raw[:, k, :],
                                                xs[:, k, 0:T].bitcast(F32), ALU.subtract)\
                            .then_inc(p_ready, 1)
                if s.name == "gate":
                    feed(feeds, f"g_ple_in{l}", (o_buf, f"g_post{l}", l, "out"))
                    feeds += 1

                def first(i, j):
                    if s.name in ("window", "conv", "latent", "gate") and isinstance(i, int) and i == j == 0:
                        which = "ple" if s.name == "gate" else "enter"
                        norm(l, which, rstd_x)
                    m = i * s.width + j
                    v = val[:, j % 4, :]
                    if s.name == "window":
                        read_bank(s, i, j, v)
                        wait(ve, pool_done, m + (s.base["p"] - 3))
                        nc.vector.tensor_tensor(win[:, j % 4, PAD:], v, rstd_x[:], ALU.mult)\
                            .then_inc(val_ready, 1)
                    elif s.name == "pooled":
                        read_bank(s, i, j, v)
                        nc.vector.tensor_scalar(wide[:, m, :], v, col("pool_b", m),
                                                col("pool_scale", m), ALU.add, ALU.mult)
                    elif s.name in ("silu", "gate", "za", "zc", "zb", "vb", "ub", "latent"):
                        if s.name in ("latent", "vb", "ub"):
                            wait(ve, pool_done if s.name == "latent" else inner_ready,
                                 (s.base["p"] if s.name == "latent" else gelus * 8) + m - 3)
                        read_bank(s, i, j, v)
                        nc.vector.tensor_tensor(v, v, rstd_x[:], ALU.mult).then_inc(val_ready, 1)
                    elif s.name in ("rope_k", "gqk", "gv", "uq", "ukv"):
                        read_bank(s, i, j, v)
                        dest = {"rope_k": ka, "gqk": gqk, "gv": v_raw, "uq": q_buf, "ukv": k_buf}[s.name]
                        if s.name == "ukv" and m >= 8:
                            dest, m = v_raw, m - 8
                        dest = dest if s.name == "rope_k" else dest[:, m, :]
                        r_ = {"uq": rstd_r, "ukv": rstd_kv}.get(s.name, rstd_x)
                        nc.vector.tensor_tensor(dest, v, r_[:], ALU.mult).then_inc(val_ready, 1)
                    elif s.name == "mix":
                        pair, q = i * (s.width // 2) + j // 2, j // 2
                        v, a = val[:, 2 * (q % 2) + j % 2, :], act[:, q % 2, :]
                        if j % 2 == 0:
                            read_bank(s, i, j, v)
                            nc.vector.tensor_tensor(v, v, rstd_x[:], ALU.mult).then_inc(val_ready, 1)
                            return
                        m, branch = i * 4 + q // 3, q % 3
                        sum_ = act[:, 2 + (q // 3) % 2, :]
                        ve.wait_ge(act_ready, pair + (s.base["t"] + 1))
                        nc.vector.tensor_scalar(a, a, 0.5, 0.5, ALU.mult, ALU.add)
                        read_bank(s, i, j, v)
                        if branch == 0:
                            wait(ve, pool_done, m + (s.base["p"] - 1))
                            link(nc.vector.tensor_tensor(sum_, v, a, ALU.mult))
                        else:
                            link(nc.vector.tensor_tensor(v, v, a, ALU.mult))
                            ins = nc.vector.tensor_tensor(sum_, sum_, v, ALU.add)
                            if branch == 1:
                                link(ins)
                            else:
                                ins.then_inc(res_ready, 1)
                    elif s.name == "wo":
                        read_bank(s, i, j, v)
                        nc.vector.tensor_tensor(x_buf[:, m, :], x_buf[:, m, :], v, ALU.add)\
                            .then_inc(res_ready, 1)
                    elif s.name == "squared":
                        read_bank(s, i, j, o_buf[:, m, :])
                    elif s.name == "plain":
                        read_bank(s, i, j, gated[:, m, :])
                    elif s.name == "conv":
                        read_bank(s, i, j, v)
                        x_ = taps_in[:, j % 2, :]
                        link(nc.vector.tensor_tensor(x_[:, PAD:], v, rstd_x[:], ALU.mult))
                        o_ = wide[:, m, :]
                        link(nc.vector.tensor_scalar(o_, x_[:, PAD:], col(f"conv_w{TAPS - 1}", m),
                                                     col("conv_b", m), ALU.mult, ALU.add))
                        for tap in range(TAPS - 1):
                            at = PAD - (TAPS - 1) + tap
                            ins = nc.vector.scalar_tensor_tensor(
                                out=o_, in0=x_[:, at:at + T], scalar=col(f"conv_w{tap}", m), in1=o_,
                                op0=ALU.mult, op1=ALU.add)
                            if tap < TAPS - 2:
                                link(ins)
                        ins.then_inc(res_ready, 1)

                def second(i, j):
                    m = i * s.width + j
                    v, a = val[:, j % 4, :], act[:, j % 4, :]
                    if s.name == "window":
                        ve.wait_ge(pool_done, m + (s.base["p"] + 1))
                        link(nc.vector.tensor_copy(inner[:, m, 0:T], a))
                        nc.vector.tensor_tensor(inner[:, m, T:2 * T], a,
                                                inner[:, m, 0:T].bitcast(F32), ALU.subtract)\
                            .then_inc(tile_split, 1)
                    elif s.name == "latent":
                        ve.wait_ge(act_ready, m + (s.base["t"] + 1))
                        nc.vector.scalar_tensor_tensor(
                            out=latent[:, m, T:2 * T], in0=v,
                            scalar=col(("cq_g%d" if m < 4 else "ckv_g%d") % (l - 2), m % 4),
                            in1=latent[:, m, 0:T].bitcast(F32), op0=ALU.mult, op1=ALU.subtract)\
                            .then_inc(res_ready, 1)
                    elif s.name in ("silu", "za", "zc", "zb"):
                        y = {"silu": wide, "za": q_buf, "zc": g_o, "zb": s_mix}[s.name]
                        ve.wait_ge(act_ready, m + (s.base["t"] + 1))
                        link(nc.vector.scalar_tensor_tensor(out=a, in0=a, scalar=1.0, in1=v,
                                                            op0=ALU.add, op1=ALU.mult))
                        nc.vector.scalar_tensor_tensor(out=a, in0=a, scalar=0.5, in1=y[:, m, :],
                                                       op0=ALU.mult, op1=ALU.mult).then_inc(res_ready, 1)
                    elif s.name == "gate":
                        ve.wait_ge(act_ready, m + (s.base["t"] + 1))
                        link(nc.vector.tensor_scalar(a, a, 0.5, 0.5, ALU.mult, ALU.add))
                        nc.vector.tensor_tensor(gated[:, m, :], gated[:, m, :], a, ALU.mult)\
                            .then_inc(res_ready, 1)

                def gelu(m):
                    v, a = val[:, m % 4, :], act[:, m % 4, :]
                    ve.wait_ge(act_ready, m + (s.base["t"] + 1))
                    link(nc.vector.scalar_tensor_tensor(out=a, in0=a, scalar=1.0, in1=v,
                                                        op0=ALU.add, op1=ALU.mult))
                    if s.name == "vb":
                        ins = nc.vector.tensor_scalar(s_v[:, m, :], a, 0.5, None, ALU.mult)
                    else:
                        ins = nc.vector.scalar_tensor_tensor(
                            out=s_mix[:, m, :], in0=a, scalar=0.5, in1=s_mix[:, m, :], op0=ALU.mult,
                            op1=ALU.mult)
                    ins.then_inc(res_ready, 1)

                def gates(i, h):
                    t, m = i * 4 + h, i * 8 + 2 * h
                    ve.wait_ge(lru_sig, t * 4 + 4)
                    link(nc.vector.tensor_scalar(lru_act[:, :, :], lru_act[:, :, :], 0.5, 0.5,
                                                 ALU.mult, ALU.add))
                    for j in range(2):
                        d = decay[:, bass.ds(m + j, 1)] if not isinstance(m, int) else \
                            decay[:, m + j:m + j + 1]
                        ins = nc.vector.tensor_scalar(val[:, j, :], lru_act[:, j, :], d, None, ALU.mult)
                    ins.then_inc(lru_p, 1)

                def one_minus_a2(i, h):
                    t = i * 4 + h
                    ve.wait_ge(lru_at, t * 2 + 2)
                    link(nc.vector.tensor_tensor(val[:, 0:2, :], lru_a[:, :, :], lru_a[:, :, :], ALU.mult))
                    nc.vector.scalar_tensor_tensor(out=lru_act[:, 0:2, :], in0=val[:, 0:2, :], scalar=1.0,
                                                   in1=lru_act[:, 0:2, :], op0=ALU.add, op1=ALU.mult)\
                        .then_inc(lru_m, 1)

                def scan(i, h):
                    t, m = i * 4 + h, i * 8 + 2 * h
                    ve.wait_ge(lru_b, t + 1)
                    for j in range(2):
                        ins = nc.vector.tensor_tensor_scan(
                            out=wide[:, m + j, :], data0=lru_a[:, j, :], data1=lru_act[:, j, :],
                            initial=0.0, op0=ALU.mult, op1=ALU.add)
                    ins.then_inc(lru_y, 1)
                    ve.wait_ge(lru_y, t + 1)

                def read_z(i, h, j):
                    v = act[:, 2 + j, :]
                    read_bank(s, i, 6 * h + 4 + j, v)
                    nc.vector.tensor_tensor(v, v, rstd_x[:], ALU.mult).then_inc(val_ready, 1)

                def finish_z(i, h, j):
                    z = i * 8 + 2 * h + j
                    ve.wait_ge(act_ready, z + (s.base["t"] + 1))
                    a, v = act[:, j, :], act[:, 2 + j, :]
                    link(nc.vector.scalar_tensor_tensor(out=a, in0=a, scalar=1.0, in1=v,
                                                        op0=ALU.add, op1=ALU.mult))
                    nc.vector.scalar_tensor_tensor(out=a, in0=a, scalar=0.5, in1=wide[:, z, :],
                                                   op0=ALU.mult, op1=ALU.mult).then_inc(res_ready, 1)

                def lru_unit(i, u):
                    h, q = divmod(u, 5)
                    last = None if isinstance(i, int) and i == h == 0 else (i, h - 1) if h else (i - 1, 3)
                    if q == 0:
                        if last:
                            scan(*last)
                        for j in range(4):
                            read_bank(s, i, 6 * h + j, val[:, j, :])
                    elif q == 1:
                        if last:
                            finish_z(*last, 0)
                        gates(i, h)
                        if last:
                            finish_z(*last, 1)
                    elif q == 2:
                        one_minus_a2(i, h)
                        read_z(i, h, 0)
                    elif q == 4:
                        read_z(i, h, 1)

                def turn(i):
                    for u in range(s.units):
                        n_ = s.unit0 + u + LOOKAHEAD
                        split_lo(i * s.units + n_, n_ % SLOTS)
                        if s.name == "lru":
                            lru_unit(i, u)
                            continue
                        for j, p in enumerate(s.products):
                            if p.last_unit == u:
                                first(i, j)
                                if s.name in ("vb", "ub"):
                                    if i * s.width + j >= 2:
                                        gelu(i * s.width + j - 2)
                                elif not (isinstance(i, int) and i == 0 and j == 0):
                                    second(*before(s, i, j))

                per = {"window": 4, "silu": 4, "gate": 4, "conv": 16, "lru": 16, "za": 4, "zc": 4,
                       "zb": 4, "mix": 4 * 4}.get(s.name, 0)
                run_stage(ve, s, turn, per, dve_chain)
                if s.name == "lru":
                    scan(s.turns - 1, 3)
                    finish_z(s.turns - 1, 3, 0)
                    finish_z(s.turns - 1, 3, 1)
                elif s.name in ("window", "silu", "gate", "latent", "za", "zc", "zb"):
                    second(s.turns - 1, s.width - 1)
                elif s.name in ("vb", "ub"):
                    gelu(6)
                    gelu(7)
                    gelus += 1
                if s.name == "rope_k":
                    norm(l, "cq", rstd_r)
                    norm(l, "ckv", rstd_kv)
                if s.name == "gqk":
                    gla_bias(l - 2)
                if s.name == "gv":
                    gla(l - 2)
                if s.name == "ukv":
                    attention(l - 2)
                if s.name == "vb":
                    spatial_gate(l - 2)

        @block.gpsimd
        def _(gp):
            link = lambda ins: pool_chain.link(gp, ins)

            def feed(f):
                for b in range(4):
                    gp.wait_ge(x_sq, f * 4 + b + 1)
                    if b == 0:
                        ins = nc.gpsimd.tensor_copy(act[:, :, :], val[:, :, :])
                    else:
                        ins = nc.gpsimd.tensor_tensor(act[:, :, :], act[:, :, :], val[:, :, :], ALU.add)
                    ins.then_inc(sq_added, 1)
                    gp.wait_ge(sq_added, f * 4 + b + 1)

            def split(dest, source):
                link(nc.gpsimd.tensor_copy(dest[:, 0:T], source))
                nc.gpsimd.tensor_tensor(dest[:, T:2 * T], source, dest[:, 0:T].bitcast(F32),
                                        ALU.subtract).then_inc(pool_done, 1)

            gp.wait_ge(consts_ready, 1)
            gp.wait_ge(consts_in, 32)
            feeds = 0
            for n, s in enumerate(stages):
                l = s.layer
                if s.name in ("window", "conv"):
                    feed(feeds)
                    feeds += 1
                if s.name == "gate":
                    feed(feeds)
                    feeds += 1
                if s.name == "latent":
                    feed(feeds)
                    feeds += 1
                    if l == 2:
                        gp.wait_ge(rope_done, 2)
                    link(nc.gpsimd.memset(acc_kv[:], 0.0))
                if s.name in ("squared", "gate", "latent", "vb"):
                    before_ = {"squared": "out", "gate": "gate", "latent": "cq"}
                    if s.name == "vb":
                        gp.wait_ge(ms_ready, norms[l, "cq"] + 1)
                    else:
                        wait(gp, ms_ready, norms[l, before_[s.name]])
                    wait(gp, sgu_ms, l - 2)
                    link(nc.gpsimd.memset(acc[:], 0.0))

                def post(i, j, group=None):
                    m = i * (4 if s.name == "mix" else s.width) + j
                    wait(gp, pool_done, m + s.base["p"])
                    if s.name == "window":
                        x_ = win[:, j % 4, :]
                        gp.wait_ge(val_ready, m + (s.base["v"] + 1))
                        wait(gp, tile_split, m - 3)
                        src = x_
                        for level in range(group + 1):
                            dst = win[:, 4 + level % 2, :]
                            back = PAD - (1 << level)
                            link(nc.gpsimd.tensor_tensor(dst[:, PAD:], src[:, PAD:],
                                                         src[:, back:back + T], ALU.add))
                            src = dst
                        link(nc.gpsimd.tensor_tensor(src[:, PAD:], src[:, PAD:],
                                                     inv_count[:, group, :], ALU.mult))
                        nc.gpsimd.tensor_tensor(act[:, j % 4, :], src[:, PAD:], x_[:, PAD:],
                                                ALU.subtract).then_inc(pool_done, 1)
                    elif s.name in ("silu", "za", "zc", "zb"):
                        gp.wait_ge(res_ready, m + (s.base["q"] + 1))
                        first_tile = {"za": 0, "zb": 8, "zc": 16}.get(s.name)
                        split(inner[:, m, :] if s.name == "silu" else y_abc[:, m + first_tile, :],
                              act[:, j % 4, :])
                    elif s.name == "mix":
                        gp.wait_ge(res_ready, m + (s.base["q"] + 1))
                        split(merged[:, m, :], act[:, 2 + j % 2, :])
                    elif s.name == "latent":
                        gp.wait_ge(val_ready, m + (s.base["v"] + 1))
                        a, sum_ = val[:, j % 4, :], (acc if m < 4 else acc_kv)[:]
                        link(nc.gpsimd.tensor_tensor(sq[:], a, a, ALU.mult))
                        nc.gpsimd.tensor_tensor(sum_, sum_, sq[:], ALU.add).then_inc(pool_done, 1)
                        gp.wait_ge(pool_done, m + (s.base["p"] + 1))
                    elif s.name == "conv":
                        gp.wait_ge(res_ready, m + (s.base["q"] + 1))
                        split(inner[:, m, :], wide[:, m, :])
                    elif s.name in ("squared", "gate"):
                        if s.name == "squared":
                            gp.wait_ge(bank_free, bank_of(s, i, j) + 1)
                            a = o_buf[:, m, :]
                        else:
                            gp.wait_ge(res_ready, m + (s.base["q"] + 1))
                            a = gated[:, m, :]
                        link(nc.gpsimd.tensor_tensor(sq[:], a, a, ALU.mult))
                        nc.gpsimd.tensor_tensor(acc[:], acc[:], sq[:], ALU.add).then_inc(pool_done, 1)
                        gp.wait_ge(pool_done, m + (s.base["p"] + 1))

                def turn(i):
                    if s.name == "lru":
                        for h in range(4):
                            t, m = i * 4 + h, i * 8 + 2 * h
                            gp.wait_ge(lru_root, t + 1)
                            b_ = lru_act[:, 0:2, :]
                            link(nc.gpsimd.tensor_tensor(b_, b_, lru_act[:, 2:4, :], ALU.mult))
                            nc.gpsimd.tensor_tensor(b_, b_, wide[:, bass.ds(m, 2), :]
                                                    if not isinstance(m, int) else wide[:, m:m + 2, :],
                                                    ALU.mult).then_inc(lru_b, 1)
                            for j in range(2):
                                z = m + j
                                wait(gp, pool_done, z + s.base["p"])
                                gp.wait_ge(res_ready, z + (s.base["q"] + 1))
                                split(inner[:, z, :], act[:, j, :])
                    elif s.name in ("vb", "ub"):
                        for j in range(s.width):
                            gelu_inner(i * s.width + j)
                            if s.name == "vb" and i * s.width + j >= 2:
                                square_v(i * s.width + j - 2)
                    else:
                        for j in range(4 if s.name == "mix" else s.width):
                            post(i, j)

                def gelu_inner(m):
                    v, a = val[:, m % 4, :], act[:, m % 4, :]
                    gp.wait_ge(val_ready, m + (s.base["v"] + 1))
                    wait(gp, res_ready, m + (s.base["q"] - 3))
                    link(nc.gpsimd.tensor_tensor(a, v, v, ALU.mult))
                    link(nc.gpsimd.tensor_scalar(a, a, GELU_C, 1.0, ALU.mult, ALU.add))
                    nc.gpsimd.tensor_tensor(a, a, v, ALU.mult).then_inc(inner_ready, 1)

                def square_v(m):
                    gp.wait_ge(res_ready, m + (s.base["q"] + 1))
                    wait(gp, pool_done, m + s.base["p"])
                    link(nc.gpsimd.tensor_tensor(sq[:], s_v[:, m, :], s_v[:, m, :], ALU.mult))
                    nc.gpsimd.tensor_tensor(acc[:], acc[:], sq[:], ALU.add).then_inc(pool_done, 1)

                if s.name == "window":
                    for group in range(4):
                        def group_turn(i):
                            for j in range(4):
                                post(i, j, group)
                        if group == 0:
                            group_turn(0)
                            group_turn(1)
                        else:
                            with gp.Fori(2 * group, 2 * group + 2) as i:
                                with pool_chain.loop(i - 2 * group, 2, 4 * (group + 2)):
                                    group_turn(i)
                elif s.name not in ("pooled", "plain", "rope_k", "gqk", "gv", "uq", "ukv", "wo"):
                    run_stage(gp, s, turn, 12 if s.name == "lru" else 4, pool_chain)
                if s.name == "vb":
                    square_v(6)
                    square_v(7)
                    gp.wait_ge(sgu_var, l - 1)
                    nc.gpsimd.tensor_tensor(s_rstd, s_col, power[:, 0:1].broadcast_to([P, 2]), ALU.pow)\
                        .then_inc(sgu_rstd, 1)
                if s.name == "ukv":
                    gp.wait_ge(att_roped, l - 1)
                    for h in range(A_HEADS):
                        g, grp = (l - 2) * A_HEADS + h, h // 4
                        if h >= 2:
                            gp.wait_ge(att_scores, g - 1)
                        at = TABLE["sel"].start + h % 4
                        nc.gpsimd.tensor_scalar(qm[h % 2], q_buf[:, 8 + 2 * grp:10 + 2 * grp, :],
                                                tab[:, at:at + 1], None, ALU.mult).then_inc(att_qm, 1)
                if s.name == "gv":
                    for n in range(2 * G_HEADS):
                        gp.wait_ge(gla_q, (l - 2) * 2 * G_HEADS + n + 1)
                        d = g_d[n % 2]
                        nc.gpsimd.tensor_tensor(
                            d, d, gqk[:, 4 + n // 2:5 + n // 2, :].broadcast_to([P, 4, T]), ALU.mult)\
                            .then_inc(gla_k, 1)


def feature_major(a):
    t, f = a.shape
    return a.reshape(t, f // P, P).transpose(2, 1, 0)


def tiles(w):
    k, n = w.shape
    return w.reshape(k // P, P, n // P, P).transpose(2, 0, 1, 3)


def stream(parts):
    flat = np.concatenate([p.reshape(-1, P, P) for p in parts])
    return np.ascontiguousarray(flat.reshape(-1, UNIT_TILES, P, P).transpose(0, 2, 1, 3)
                                .reshape(-1, P, UNIT))


def constant_tables():
    i = np.arange(P)
    t = {"ident": np.eye(P)}
    masks = []
    for level in list(range(1, LEVELS)) + [0]:
        if level == 0:
            m = i[:, None] == i[None]
        else:
            half = i >> (level - 1)
            m = ((half[:, None] + 1) == half[None]) & (half[:, None] % 2 == 0)
        masks.append(m * G_DK ** -0.5)
    t["masks"] = np.concatenate(masks, 1)
    t["tri"] = i[:, None] <= i[None]
    t["neg"] = np.where(i[:, None] >= i[None], 0.0, NEG)
    t["sel"] = (i[:, None] // 32) == np.arange(4)[None]
    t["rep1"] = (i[:, None] < 32) & (i[:, None] == i[None] % 32)
    t["rep2"] = (i[:, None] >= 32) & (i[:, None] < 64) & (i[:, None] - 32 == i[None] % 32)
    t["rope_rows"] = np.repeat(i[:, None] < ROPE, 4, 1)
    exps = np.arange(0, ROPE, 2, dtype=np.float32) / np.float32(ROPE)
    t["inv_freq"] = np.tile(np.float32(1.0) / np.float32(10000.0) ** exps, 4)[:, None]
    return np.ascontiguousarray(
        np.concatenate([np.broadcast_to(t[k], (P, n)) for k, n in TABLES], 1).astype(np.float32))


def kernel(**inputs):
    import concourse.bacc as bacc
    from concourse.bass_utils import run_bass_kernel_spmd

    a = {k: np.asarray(v) for k, v in inputs.items()}
    parts = []
    for l in range(2):
        w_u, w_z = tiles(a["w_in"][l][:, :DI]), tiles(a["w_in"][l][:, DI:])
        parts.append(w_u)
        if l == 0:
            parts += [tiles(a["pool_w"][0, g]) for g in range(4)]
            parts.append(w_z)
        else:
            for h in range(HEADS):
                parts += [tiles(a["lru_wa"][0, h]), tiles(a["lru_wx"][0, h]), w_z[2 * h:2 * h + 2]]
        parts += [tiles(a["w_out"][l]), tiles(a["w_ple"][l]), tiles(a["w_ple_gate"][l])]
    sizes = (RANK, RANK, ROPE, 1024, 1024, 1024, 1024, 512, 512, 1024, 16, 1024, 3 * D)
    starts = np.cumsum((0,) + sizes)
    names = ("cq", "ckv", "kr", "za", "ub", "vb", "zb", "gq", "gk", "gv", "ar", "zc", "gate")
    part = {n: slice(starts[i], starts[i + 1]) for i, n in enumerate(names)}
    for l in range(2):
        w = a["w_in_2"][l]
        kr_ar = np.concatenate([w[:, part["kr"]], w[:, part["ar"]], np.zeros((D, 48), np.float32)], 1)
        parts += [tiles(w[:, part["cq"]]), tiles(w[:, part["ckv"]]), tiles(kr_ar),
                  tiles(w[:, part["gq"]]), tiles(w[:, part["gk"]]), tiles(w[:, part["gv"]])]
        w_q = a["mla_w_uq_2"][l].reshape(RANK, A_HEADS, QK)
        half = ROPE // 2
        parts.append(tiles(np.concatenate(
            [w_q[:, :, :NOPE].reshape(RANK, -1)]
            + [w_q[:, g:g + 4, at:at + half].reshape(RANK, -1)
               for g in (0, 4) for at in (NOPE, NOPE + half)], 1)))
        w_kv = a["mla_w_ukv_2"][l].reshape(RANK, A_HEADS, 2 * P)
        parts.append(tiles(np.concatenate([w_kv[:, :, :P].reshape(RANK, -1),
                                           w_kv[:, :, P:].reshape(RANK, -1)], 1)))
        parts += [tiles(w[:, part[n]]) for n in ("za", "zc", "vb", "ub", "zb")]
        gates = tiles(w[:, part["gate"]]).reshape(3, ND, ND, P, P)
        branches = [tiles(a["w_branch_2"][l, b]) for b in range(3)]
        for m in range(ND):
            for b in range(3):
                parts += [gates[b, m], branches[b][m]]
        parts.append(tiles(a["w_out_2"][l]))
    weights = stream(parts)

    def columns(v):
        return v.reshape(-1, P).T

    named = {}
    for l in range(2):
        for k in ("g_pre", "g_post", "g_ple_in", "g_ple_out"):
            named[f"{k}{l}"] = a[k][l]
    for k in ("pool_b", "pool_scale", "conv_b", "lru_ba", "lru_bx", "lru_L"):
        named[k] = a[k][0]
    for k in range(TAPS):
        named[f"conv_w{k}"] = a["conv_w"][0, k]
    for l in range(2):
        named[f"norm_g{l}"] = a["norm_g_2"][l]
        named[f"cq_g{l}"], named[f"ckv_g{l}"] = a["mla_cq_norm_2"][l], a["mla_ckv_norm_2"][l]
        named[f"v_g{l}"], named[f"o_g{l}"] = a["sgu_v_norm_2"][l], a["gla_o_norm_2"][l]
        named[f"b_a{l}"] = a["gla_b_a_2"][l]
        for k, g in (("q", a["mla_q_norm_2"][l]), ("k", a["mla_k_norm_2"][l])):
            named[f"g{k}_nope{l}"] = g[:NOPE]
            named[f"g{k}_r1{l}"] = np.tile(g[NOPE:NOPE + ROPE // 2], 4)
            named[f"g{k}_r2{l}"] = np.tile(g[NOPE + ROPE // 2:], 4)
    w_a2 = np.zeros((2, P, 512), np.float32)
    w_a2[:, ROPE:ROPE + 16] = a["gla_w_a2_2"]
    channels = np.ascontiguousarray(np.concatenate([columns(named[k]) for k, _ in CHANNELS], 1))
    counts = np.stack([1.0 / np.minimum(np.arange(1, T + 1), w) for w in POOL_WINDOWS])
    arrays = {
        "weights": weights,
        "x_in": np.ascontiguousarray(feature_major(a["x"][0])),
        "p_in": np.ascontiguousarray(np.stack([feature_major(a["p"][l, 0]) for l in range(2)])),
        "channels": channels,
        "tables": constant_tables(),
        "positions": np.ascontiguousarray(np.broadcast_to(a["positions_2"][0], (P, T))),
        "w_a2": w_a2,
        "w_s": np.ascontiguousarray(a["sgu_w_s_2"].transpose(0, 3, 1, 2)),
        "b_s": np.ascontiguousarray(np.broadcast_to(a["sgu_b_s_2"][:, None], (2, P, S_GROUPS, P))),
        "inv_counts": np.ascontiguousarray(
            np.broadcast_to(counts.astype(np.float32)[None], (P, 4, T))),
    }
    nc = bacc.Bacc("TRN2", target_bir_lowering=False, num_devices=1)
    order = ("weights", "x_in", "p_in", "channels", "inv_counts", "tables", "positions", "w_a2", "w_s",
             "b_s")
    aps = [nc.dram_tensor(k, arrays[k].shape, mybir.dt.from_np(arrays[k].dtype),
                          kind="ExternalInput").ap() for k in order]
    scratch = nc.dram_tensor("x_scratch", (P, ND, T), F32, kind="Internal").ap()
    out = nc.dram_tensor("out_x", (P, ND, T), F32, kind="ExternalOutput").ap()
    build(nc, *aps, scratch, out)
    r = run_bass_kernel_spmd(nc, [arrays], core_ids=[0])
    got = r.results[0]["out_x"]
    return np.ascontiguousarray(got.transpose(2, 1, 0)).reshape(1, T, D)
```
